# Optimizing a Trainium2 kernel written in Bass

```python
import jax, jax.numpy as jnp
from jax import lax
import numpy as np

D_MODEL = 1024
BATCH = 1
SEQ = 512
DEPTH = 1
DEC_BATCH = 1
DEC_SEQ = 32
PAST_LEN = 256

CHUNK = 64
POOL_WIDTH = 512
POOL_GROUPS = 4
POOL_GROUP_DIM = POOL_WIDTH // POOL_GROUPS
POOL_WINDOWS = (2, 4, 8, 16)
POOL_STATE = max(POOL_WINDOWS) - 1
SB_HEADS = 8
SB_HEAD_DIM = 64
SB_WIDTH = SB_HEADS * SB_HEAD_DIM
Q_BLOCK = 128
D_FF = 4 * D_MODEL
PLE_DIM = 256
IN_WIDTH = POOL_WIDTH + 3 * SB_WIDTH + 2 * D_MODEL
EPS = 1e-6

kernel_name = "stickbreak_pool_hybrid_step"

def rms_norm(x, g):
    xf = x.astype(jnp.float32)
    y = xf * lax.rsqrt(jnp.mean(xf * xf, axis=-1, keepdims=True) + EPS)
    return (y * g.astype(jnp.float32)).astype(x.dtype)

def multiscale_pool(u_hist, u, w_grp, scale):
    B, P, _ = u_hist.shape
    T = u.shape[1]
    full = jnp.concatenate([u_hist, u], axis=1)
    cs = jnp.cumsum(full.astype(jnp.float32), axis=1)
    cs = jnp.pad(cs, ((0, 0), (1, 0), (0, 0)))
    cs = cs.reshape(B, P + T + 1, POOL_GROUPS, POOL_GROUP_DIM)
    windows = jnp.array(POOL_WINDOWS, dtype=jnp.int32)
    end = P + 1 + jnp.arange(T, dtype=jnp.int32)
    start = jnp.maximum(end[:, None] - windows[None, :], 0)
    count = (end[:, None] - start).astype(jnp.float32)
    g_idx = jnp.arange(POOL_GROUPS, dtype=jnp.int32)
    cs_end = cs[:, end]
    cs_start = cs[:, start, g_idx[None, :]]
    mean = (cs_end - cs_start) / count[None, :, :, None]
    u4 = u.reshape(B, T, POOL_GROUPS, POOL_GROUP_DIM)
    y = (mean - u4.astype(jnp.float32)).astype(u.dtype)
    y = jnp.einsum('btgc,gcd->btgd', y, w_grp).reshape(B, T, POOL_WIDTH) * scale
    new_state = full[:, -POOL_STATE:]
    return y, new_state

def stick_breaking_block(q, k, v, q_pos, k_pos):
    z = jnp.einsum('bqhd,bkhd->bhqk', q.astype(jnp.float32), k.astype(jnp.float32)) * (SB_HEAD_DIM ** -0.5)
    causal = k_pos[None, :] < q_pos[:, None]
    log_not = jnp.where(causal, jax.nn.log_sigmoid(-z), 0.0)
    suffix = lax.cumsum(log_not, axis=3, reverse=True) - log_not
    a = jnp.where(causal, jnp.exp(jax.nn.log_sigmoid(z) + suffix), 0.0)
    o = jnp.einsum('bhqk,bkhd->bqhd', a, v.astype(jnp.float32))
    return o.astype(v.dtype)

def stick_breaking_prompt(q, k, v):
    B, T, H, Dh = q.shape
    nb = T // Q_BLOCK
    k_pos = jnp.arange(T, dtype=jnp.int32)
    qb = q.reshape(B, nb, Q_BLOCK, H, Dh).transpose(1, 0, 2, 3, 4)
    pos_b = k_pos.reshape(nb, Q_BLOCK)
    ob = lax.map(lambda args: stick_breaking_block(args[0], k, v, args[1], k_pos), (qb, pos_b))
    return ob.transpose(1, 0, 2, 3, 4).reshape(B, T, H, Dh)

def layer(x, p, pool_hist, k_hist, v_hist, is_prompt,
          g_mix, w_in, b_gate, w_pool_grp, pool_scale, w_pool_up, w_sb_up, w_out,
          g_mlp, w_up, w_down, g_ple, w_ple_gate, w_ple_proj):
    B, T, _ = x.shape
    P = k_hist.shape[1]
    xn = rms_norm(x, g_mix)
    h = xn @ w_in
    u, q, k, v, gates = jnp.split(
        h, [POOL_WIDTH, POOL_WIDTH + SB_WIDTH, POOL_WIDTH + 2 * SB_WIDTH, POOL_WIDTH + 3 * SB_WIDTH], axis=-1)
    gates = jax.nn.sigmoid((gates + b_gate).astype(jnp.float32)).astype(x.dtype)
    gate_a, gate_b = jnp.split(gates, 2, axis=-1)
    y_pool, pool_new = multiscale_pool(pool_hist, u, w_pool_grp, pool_scale)
    q = q.reshape(B, T, SB_HEADS, SB_HEAD_DIM)
    k = k.reshape(B, T, SB_HEADS, SB_HEAD_DIM)
    v = v.reshape(B, T, SB_HEADS, SB_HEAD_DIM)
    if is_prompt:
        o = stick_breaking_prompt(q, k, v)
    else:
        k_all = jnp.concatenate([k_hist, k], axis=1)
        v_all = jnp.concatenate([v_hist, v], axis=1)
        k_pos = jnp.arange(P + T, dtype=jnp.int32)
        q_pos = P + jnp.arange(T, dtype=jnp.int32)
        o = stick_breaking_block(q, k_all, v_all, q_pos, k_pos)
    y_sb = o.reshape(B, T, SB_WIDTH)
    merged = gate_a * (y_pool @ w_pool_up) + gate_b * (y_sb @ w_sb_up)
    x = x + merged @ w_out
    x = x + jnp.square(jax.nn.relu(rms_norm(x, g_mlp) @ w_up)) @ w_down
    x = x + jax.nn.sigmoid(rms_norm(x, g_ple) @ w_ple_gate) * (p @ w_ple_proj)
    return x, k, v, pool_new

def setup_inputs(seed: int = 0) -> dict:
    key = jax.random.key(seed)
    ks = jax.random.split(key, 24)
    f32 = jnp.float32

    def nrm(k, shape, scale):
        return jax.random.normal(k, shape, f32) * scale

    return {
        "x_prompt": nrm(ks[0], (BATCH, SEQ, D_MODEL), 1.0),
        "x_sample": nrm(ks[1], (DEC_BATCH, DEC_SEQ, D_MODEL), 1.0),
        "cache_k": nrm(ks[2], (DEPTH, DEC_BATCH, PAST_LEN, SB_HEADS, SB_HEAD_DIM), 1.0),
        "cache_v": nrm(ks[3], (DEPTH, DEC_BATCH, PAST_LEN, SB_HEADS, SB_HEAD_DIM), 1.0),
        "state_pool": nrm(ks[4], (DEPTH, DEC_BATCH, POOL_STATE, POOL_WIDTH), 1.0),
        "p_prompt": nrm(ks[5], (DEPTH, BATCH, SEQ, PLE_DIM), 1.0),
        "p_sample": nrm(ks[6], (DEPTH, DEC_BATCH, DEC_SEQ, PLE_DIM), 1.0),
        "g_mix": 1.0 + nrm(ks[7], (DEPTH, D_MODEL), 0.05),
        "w_in": nrm(ks[8], (DEPTH, D_MODEL, IN_WIDTH), D_MODEL ** -0.5),
        "b_gate": nrm(ks[9], (DEPTH, 2 * D_MODEL), 0.1),
        "w_pool_grp": nrm(ks[10], (DEPTH, POOL_GROUPS, POOL_GROUP_DIM, POOL_GROUP_DIM), POOL_GROUP_DIM ** -0.5),
        "pool_scale": 1.0 + nrm(ks[11], (DEPTH, POOL_WIDTH), 0.1),
        "w_pool_up": nrm(ks[12], (DEPTH, POOL_WIDTH, D_MODEL), POOL_WIDTH ** -0.5),
        "w_sb_up": nrm(ks[13], (DEPTH, SB_WIDTH, D_MODEL), SB_WIDTH ** -0.5),
        "w_out": nrm(ks[14], (DEPTH, D_MODEL, D_MODEL), D_MODEL ** -0.5),
        "g_mlp": 1.0 + nrm(ks[15], (DEPTH, D_MODEL), 0.05),
        "w_up": nrm(ks[16], (DEPTH, D_MODEL, D_FF), D_MODEL ** -0.5),
        "w_down": nrm(ks[17], (DEPTH, D_FF, D_MODEL), D_FF ** -0.5),
        "g_ple": 1.0 + nrm(ks[18], (DEPTH, D_MODEL), 0.05),
        "w_ple_gate": nrm(ks[19], (DEPTH, D_MODEL, D_MODEL), D_MODEL ** -0.5),
        "w_ple_proj": nrm(ks[20], (DEPTH, PLE_DIM, D_MODEL), PLE_DIM ** -0.5),
        "g_final": 1.0 + nrm(ks[21], (D_MODEL,), 0.05),
    }

def reference(x_prompt, x_sample, cache_k, cache_v, state_pool, p_prompt, p_sample,
              g_mix, w_in, b_gate, w_pool_grp, pool_scale, w_pool_up, w_sb_up, w_out,
              g_mlp, w_up, w_down, g_ple, w_ple_gate, w_ple_proj, g_final):
    xp, xs = x_prompt, x_sample
    empty_pool = jnp.zeros((xp.shape[0], 0, POOL_WIDTH), xp.dtype)
    empty_kv = jnp.zeros((xp.shape[0], 0, SB_HEADS, SB_HEAD_DIM), xp.dtype)
    kp_l, vp_l, pp_l, ks_l, vs_l, ps_l = [], [], [], [], [], []
    for d in range(DEPTH):
        weights = (g_mix[d], w_in[d], b_gate[d], w_pool_grp[d], pool_scale[d], w_pool_up[d], w_sb_up[d],
                   w_out[d], g_mlp[d], w_up[d], w_down[d], g_ple[d], w_ple_gate[d], w_ple_proj[d])
        xp, kp, vp, pp = layer(xp, p_prompt[d], empty_pool, empty_kv, empty_kv, True, *weights)
        xs, ksm, vsm, psm = layer(xs, p_sample[d], state_pool[d], cache_k[d], cache_v[d], False, *weights)
        kp_l.append(kp); vp_l.append(vp); pp_l.append(pp)
        ks_l.append(ksm); vs_l.append(vsm); ps_l.append(psm)
    y_prompt = rms_norm(xp, g_final)
    y_sample = rms_norm(xs, g_final)
    k_prompt = jnp.stack(kp_l); v_prompt = jnp.stack(vp_l); pool_prompt = jnp.stack(pp_l)
    k_sample = jnp.stack(ks_l); v_sample = jnp.stack(vs_l); pool_sample = jnp.stack(ps_l)
    return (y_prompt, y_sample, k_prompt, v_prompt, pool_prompt, k_sample, v_sample, pool_sample)


_drawn_inputs = setup_inputs


def setup_inputs(seed=0):
    import zlib

    import numpy as np

    out = dict(_drawn_inputs(seed))
    spreads = {}
    factors = {'b_gate': 2.691, 'g_ple': 23.213}
    for name, (base, spread) in spreads.items():
        noise = np.random.default_rng([zlib.crc32(name.encode()), seed]).standard_normal(out[name].shape)
        drawn = base * np.exp(spread * noise) if base else spread * noise
        out[name] = __import__('jax').numpy.asarray(drawn.astype(out[name].dtype))
    for name, factor in factors.items():
        out[name] = (out[name] * factor).astype(out[name].dtype)
    return out
```

```python
from contextlib import ExitStack

import numpy as np

import concourse.bass as bass
from concourse import mybir

ALU = mybir.AluOpType
ACT = mybir.ActivationFunctionType
F32 = mybir.dt.float32
F32R = mybir.dt.float32r

P = 128
D_MODEL = 1024
SEQ = 512
DEC = 32
PAST = 256
TOK = SEQ + DEC
HALF = TOK // 2
HEADS = 8
DH = 64
PAIRS = HEADS * DH // P
GROUPS = 4
WINDOWS = (2, 4, 8, 16)
STATE = max(WINDOWS) - 1
D_FF = 4 * D_MODEL
PLE = 256
EPS = 1e-6
KT = D_MODEL // P
QB = SEQ // P

S1_PER = 8
T_MIX = PAIRS * S1_PER
T_OUT = T_MIX + KT
T_MLP = T_OUT + KT
CHUNKS = D_FF // D_MODEL
MLP_PER = 2 * KT
T_PLE = T_MLP + CHUNKS * MLP_PER
N_TILES = T_PLE + KT
W_RING = 4
RAW_RING = 2
AHEAD = W_RING - 1

N_VS = T_MIX
N_GRP = N_VS + 1
N_MIX = N_GRP + GROUPS
N_OUT = N_MIX + 2 * KT
N_STAT1 = N_OUT + KT
N_MLP = N_STAT1 + 1
N_STAT2 = N_MLP + CHUNKS * MLP_PER
N_PLE = N_STAT2 + 1
N_STAT3 = N_PLE + 2 * KT

Z_OFF = (0, 512, 1024, 896)
Z_LEN = tuple(SEQ - P * b for b in range(QB))
Z_COLS = sum(Z_LEN)
ZS = HEADS * DEC
PADW = STATE + SEQ + STATE + DEC
U_PROMPT = STATE
U_STATE = STATE + SEQ
U_SAMPLE = U_STATE + STATE


def result_slot(n):
    return n % 2 if n < N_MIX else n % 4


def result_before(n):
    for m in range(n - 1, -1, -1):
        if result_slot(m) == result_slot(n):
            return m
    return None


def results_by(t):
    if t < 0:
        return None
    if t < T_MIX:
        return t + 1
    if t < T_OUT:
        return N_MIX + 2 * (t - T_MIX) + 2
    if t < T_MLP:
        return N_OUT + (t - T_OUT) + 1
    if t < T_PLE:
        return N_MLP + (t - T_MLP) + 1
    return N_PLE + 2 * (t - T_PLE) + 1


def hybrid_step_kernel(nc, w_tiles, x_t, p_t, ck_t, cv, state_t, w_grp, w_ple, vecs,
                       y_t, k_t, v_t, pool_t):
    ctx = ExitStack()
    with ctx:
        def sb(name, shape, dt=F32):
            return ctx.enter_context(nc.sbuf_tensor(name, shape, dt))

        def sem(name):
            return ctx.enter_context(nc.semaphore(name))

        raw = sb("raw", [P, RAW_RING, D_MODEL])
        w_hi = sb("w_hi", [P, W_RING, KT, P], F32R)
        w_lo = sb("w_lo", [P, W_RING, KT, P], F32R)
        a_hi = sb("a_hi", [P, KT * TOK], F32R)
        a_lo = sb("a_lo", [P, KT * TOK], F32R)
        b_hi = sb("b_hi", [P, KT * TOK], F32R)
        b_lo = sb("b_lo", [P, KT * TOK], F32R)
        xt = sb("xt", [P, KT, TOK])
        gates = sb("gates", [P, 2 * KT, TOK])
        rn = sb("rn", [P, TOK])
        ev = sb("ev", [P, 3, 576])
        upad = sb("upad", [P, GROUPS, PADW])
        ysb = sb("ysb", [P, PAIRS, TOK])
        work = sb("work", [P, Z_COLS])
        ckt = sb("ckt", [P, PAIRS, PAST])
        cvn = sb("cvn", [P, PAST // P, HEADS * DH])
        qbd = sb("qbd", [P, PAIRS, 2 * DEC])
        kst = sb("kst", [P, PAIRS, DEC])
        vst = sb("vst", [P, PAIRS, DEC])
        ident = sb("ident", [P, P])
        negtri = sb("negtri", [P, P], F32R)
        negone = sb("negone", [P, P], F32R)
        vec = sb("vec", [P, 4 * KT + 2 * KT + GROUPS])
        invc = sb("invc", [P, STATE + 1])
        epsc = sb("epsc", [P, 1])
        psum = ctx.enter_context(nc.psum_tensor("psum", [P, 8, 512], F32))

        g_mix, g_mlp, g_ple, g_fin, bgate, pscale = (
            vec[:, 0:KT], vec[:, KT:2 * KT], vec[:, 2 * KT:3 * KT], vec[:, 3 * KT:4 * KT],
            vec[:, 4 * KT:6 * KT], vec[:, 6 * KT:6 * KT + GROUPS])

        def halves(ap):
            return ap.rearrange("p (a c) -> p a c", a=2)

        def cols(buf, k, lo=0, hi=TOK):
            return buf[:, k * TOK + lo:k * TOK + hi]

        def result(n):
            s = result_slot(n)
            return psum[:, 2 * s:2 * s + 2, 0:HALF]

        flat = psum[:, 4:7, :].rearrange("p a c -> p (a c)")
        z_ps = flat[:, 0:Z_COLS]
        o_ps = psum[:, 7, :]
        zs_ps = psum[:, 4, :]
        zs2_ps = psum[0:DEC, 5, 0:ZS]
        os_ps = psum[:, 6, 0:ZS]

        QOF, KOF, VOF, SOF, GOF = 0, TOK, 2 * TOK, 2 * TOK + SEQ, KT * TOK - GROUPS * P
        assert SOF + Z_COLS <= GOF
        work_s = work[:, 0:2 * ZS]
        work_s2 = work[0:DEC, 2 * ZS:3 * ZS]
        vsn = work[0:DEC, 3 * ZS:3 * ZS + HEADS * DH]
        acc = work[:, 0:TOK]
        var = work[:, TOK:2 * TOK]
        p_raw = gates[:, 0:2, :]
        wp_raw = gates[:, 2:6, 0:SEQ]
        pr_of, wp_of = 0, 2 * TOK

        taken = sem("taken")
        x_in = [sem(f"x_in{k}") for k in range(KT)]
        vec_in = sem("vec_in")
        grp_in = sem("grp_in")
        past_in = sem("past_in")
        state_in = sem("state_in")
        ple_in = sem("ple_in")
        raw_in = [sem(f"raw_in{s}") for s in range(RAW_RING)]
        whi_done = sem("whi_done")
        wlo_done = sem("wlo_done")
        full = sem("full")
        const_made = sem("const_made")
        base_made = sem("base_made")
        xhi_done = sem("xhi_done")
        xlo_done = sem("xlo_done")
        sq_done = sem("sq_done")
        sq_added = sem("sq_added")
        stat0 = sem("stat0")
        var_done = sem("var_done")
        root_done = sem("root_done")
        dve_own = sem("dve_own")
        act_own = sem("act_own")
        qkhi_done = sem("qkhi_done")
        qklo_done = sem("qklo_done")
        vt_done = sem("vt_done")
        vhi_done = sem("vhi_done")
        vlo_done = sem("vlo_done")
        kv_out = [sem("k_out"), sem("v_out")]
        z_done = sem("z_done")
        ln_done = sem("ln_done")
        sp_done = sem("sp_done")
        spm_done = sem("spm_done")
        shi_done = sem("shi_done")
        slo_done = sem("slo_done")
        c_done = sem("c_done")
        prob_done = sem("prob_done")
        pm_done = sem("pm_done")
        phi_done = sem("phi_done")
        plo_done = sem("plo_done")
        o_done = sem("o_done")
        y_done = sem("y_done")
        mean_done = sem("mean_done")
        mhi_done = sem("mhi_done")
        mlo_done = sem("mlo_done")
        ghi_done = sem("ghi_done")
        glo_done = sem("glo_done")
        ybhi_done = sem("ybhi_done")
        yblo_done = sem("yblo_done")
        sig_done = sem("sig_done")
        mix_done = sem("mix_done")
        bhi_done = sem("bhi_done")
        blo_done = sem("blo_done")
        res_done = sem("res_done")
        h_done = sem("h_done")
        hhi_done = sem("hhi_done")
        hlo_done = sem("hlo_done")
        pt_done = sem("pt_done")
        ptlo_done = sem("ptlo_done")
        psig_done = sem("psig_done")
        fin_done = sem("fin_done")
        out_done = sem("out_done")
        pool_out = sem("pool_out")

        block = ctx.enter_context(nc.Block())

        @block.sync
        def _(sp):
            for k in range(KT):
                sp.dma_start(xt[:, k, :], x_t[k, :, :]).then_inc(x_in[k], 16)
                if k < RAW_RING:
                    sp.dma_start(raw[:, k, :], w_tiles[k, :, :]).then_inc(raw_in[k], 16)
            with sp.Fori(1, N_TILES // RAW_RING) as r:
                for s in range(RAW_RING):
                    sp.wait_ge(wlo_done, r * RAW_RING + (s - RAW_RING + 1))
                    sp.dma_start(raw[:, s, :], w_tiles[r * RAW_RING + s, :, :]).then_inc(raw_in[s], 16)
            for k in range(KT):
                sp.wait_ge(fin_done, k + 1)
                sp.dma_start(y_t[k, :, :], xt[:, k, :]).then_inc(out_done, 16)
            sp.wait_ge(out_done, 16 * KT)

        @block.gpsimd
        def _(pool):
            pool.memset(ident[:, :], 0.0).then_inc(base_made, 1)
            pool.memset(work[:, 0:P], -1.0).then_inc(base_made, 1)
            pool.memset(work[:, P:2 * P], -1.0).then_inc(base_made, 1)
            pool.memset(epsc[:, :], EPS).then_inc(const_made, 1)
            for n in range(STATE + 1):
                pool.memset(invc[:, n:n + 1], 1.0 / (n + 1)).then_inc(const_made, 1)
            pool.memset(qbd[:, :, :], 0.0).then_inc(const_made, 1)
            pool.memset(upad[:, :, 0:STATE], 0.0).then_inc(const_made, 1)
            pool.wait_ge(base_made, 3)
            pool.affine_select(out=ident[:, :], in_=ident[:, :], compare_op=ALU.not_equal, fill=1.0,
                               base=0, pattern=[[-1, P]], channel_multiplier=1).then_inc(const_made, 1)
            pool.affine_select(out=negtri[:, :], in_=work[:, 0:P], compare_op=ALU.is_ge, fill=0.0,
                               base=0, pattern=[[-1, P]], channel_multiplier=1).then_inc(const_made, 1)
            pool.tensor_copy(negone[:, :], work[:, P:2 * P]).then_inc(const_made, 1)

            def mask_diagonals(done):
                for b in range(QB):
                    d = work[:, Z_OFF[b]:Z_OFF[b] + P]
                    pool.affine_select(out=d, in_=d, compare_op=ALU.is_gt, fill=0.0,
                                       base=0, pattern=[[1, P]], channel_multiplier=-1).then_inc(done, 1)

            for g in range(HEADS):
                pool.wait_ge(sp_done, g + 1)
                mask_diagonals(spm_done)
                pool.wait_ge(prob_done, g + 1)
                mask_diagonals(pm_done)
            new = work_s2.rearrange("p (h q) -> p h q", h=HEADS)
            for ready, done in ((sp_done, spm_done), (prob_done, pm_done)):
                pool.wait_ge(ready, HEADS + 1)
                pool.affine_select(out=new, in_=new, compare_op=ALU.is_gt, fill=0.0,
                                   base=0, pattern=[[0, HEADS], [1, DEC]], channel_multiplier=-1).then_inc(done, 1)

        N_CONST = STATE + 1 + 6

        @block.scalar
        def _(act):
            act.dma_start(vec[:, :], vecs).then_inc(vec_in, 16)
            act.dma_start(ev[:, 0, 0:GROUPS * P], w_grp).then_inc(grp_in, 16)
            act.dma_start(ckt[:, :, :], ck_t).then_inc(past_in, 16)
            act.dma_start(cvn[:, :, :], cv).then_inc(past_in, 16)
            act.dma_start(upad[:, :, U_STATE:U_SAMPLE], state_t).then_inc(state_in, 16)

            def split(t, i=0, per=0, left=None):
                if left is None:
                    left = results_by(t - W_RING)
                s = t % W_RING
                act.wait_ge(raw_in[t % RAW_RING], 16 * (t // RAW_RING + 1) + i * (16 * per // RAW_RING))
                if left:
                    act.wait_ge(full, left + i * per)
                act.activation(w_hi[:, s, :, :].rearrange("p k c -> p (k c)"), raw[:, t % RAW_RING, :],
                               ACT.Copy).then_inc(whi_done, 1)

            def scaled_input(k, g, n0):
                act.activation(cols(a_hi, k), xt[:, k, :], ACT.Copy, scale=g[:, k:k + 1]).then_inc(xhi_done, 1)
                if k >= 2:
                    act.wait_ge(sq_added, n0 + k - 1)
                act.activation(ev[:, 1 + k % 2, 0:TOK], xt[:, k, :], ACT.Square).then_inc(sq_done, 1)

            act.wait_ge(vec_in, 16)
            for k in range(KT):
                act.wait_ge(x_in[k], 16)
                scaled_input(k, g_mix, 0)
                if k < AHEAD:
                    split(k)
            act.wait_ge(grp_in, 16)
            act.activation(b_hi[:, GOF:GOF + GROUPS * P], ev[:, 0, 0:GROUPS * P], ACT.Copy).then_inc(ghi_done, 1)
            act.wait_ge(var_done, 1)
            act.activation(ev[:, 1, 0:TOK], var, ACT.Sqrt).then_inc(root_done, 1)

            def chain(hh, i):
                g = 2 * i + hh
                act.wait_ge(z_done, g + 1)
                act.activation(work[:, :], z_ps, ACT.Abs).then_inc(act_own, 1)
                act.wait_ge(act_own, 2 * g + 1)
                act.activation(work[:, :], work[:, :], ACT.Exp, scale=-1.0).then_inc(act_own, 1)
                act.wait_ge(act_own, 2 * g + 2)
                act.activation(work[:, :], work[:, :], ACT.Ln, bias=1.0).then_inc(ln_done, 1)

            def stick_hi(hh, i):
                g = 2 * i + hh
                act.wait_ge(spm_done, g * QB + QB)
                act.activation(b_hi[:, SOF:SOF + Z_COLS], work[:, :], ACT.Copy).then_inc(shi_done, 1)

            def prob(hh, i):
                g = 2 * i + hh
                act.wait_ge(c_done, g + 1)
                act.activation(work[:, :], z_ps, ACT.Exp).then_inc(prob_done, 1)

            def prob_hi(hh, i):
                g = 2 * i + hh
                act.wait_ge(pm_done, g * QB + QB)
                act.activation(b_hi[:, SOF:SOF + Z_COLS], work[:, :], ACT.Copy).then_inc(phi_done, 1)

            def pair(i):
                first = isinstance(i, int) and i == 0
                if not first:
                    prob(1, i - 1)
                split(AHEAD + 0, i, S1_PER, 0)
                if not first:
                    prob_hi(1, i - 1)
                act.wait_ge(taken, 1 + i * S1_PER)
                act.activation(b_hi[:, QOF:QOF + TOK], ev[:, 0, 0:TOK], ACT.Copy).then_inc(qkhi_done, 1)
                split(AHEAD + 1, i, S1_PER, 1)
                act.wait_ge(taken, 2 + i * S1_PER)
                act.activation(b_hi[:, KOF:KOF + TOK], ev[:, 1, 0:TOK], ACT.Copy).then_inc(qkhi_done, 1)
                act.dma_start(k_t[i, :, :], ev[:, 1, 0:TOK]).then_inc(kv_out[0], 16)
                split(AHEAD + 2, i, S1_PER, 2)
                chain(0, i)
                act.wait_ge(taken, 3 + i * S1_PER)
                act.dma_start(v_t[i, :, :], ev[:, 2, 0:TOK]).then_inc(kv_out[1], 16)
                act.wait_ge(vt_done, i + 1)
                act.activation(b_hi[:, VOF:VOF + SEQ], o_ps, ACT.Copy).then_inc(vhi_done, 1)
                split(AHEAD + 3, i, S1_PER, 3)
                stick_hi(0, i)
                split(AHEAD + 4, i, S1_PER, 4)
                prob(0, i)
                split(AHEAD + 5, i, S1_PER, 5)
                prob_hi(0, i)
                chain(1, i)
                split(AHEAD + 6, i, S1_PER, 6)
                stick_hi(1, i)
                split(AHEAD + 7, i, S1_PER, 7)

            pair(0)
            with act.Fori(1, PAIRS) as i:
                pair(i)
            prob(1, PAIRS - 1)
            prob_hi(1, PAIRS - 1)

            act.wait_ge(z_done, HEADS + 1)
            act.wait_ge(plo_done, HEADS)
            act.activation(work_s, zs_ps, ACT.Abs).then_inc(act_own, 1)
            act.activation(work_s2, zs2_ps, ACT.Abs).then_inc(act_own, 1)
            act.wait_ge(act_own, 2 * HEADS + 2)
            act.activation(work_s, work_s, ACT.Exp, scale=-1.0).then_inc(act_own, 1)
            act.activation(work_s2, work_s2, ACT.Exp, scale=-1.0).then_inc(act_own, 1)
            act.wait_ge(act_own, 2 * HEADS + 4)
            act.activation(work_s, work_s, ACT.Ln, bias=1.0).then_inc(act_own, 1)
            act.activation(work_s2, work_s2, ACT.Ln, bias=1.0).then_inc(ln_done, 1)
            act.wait_ge(y_done, HEADS)
            av = a_hi[:, 0:PAIRS * TOK].rearrange("p (k t) -> p k t", k=PAIRS)
            act.activation(av[:, :, 0:SEQ], ysb[:, :, 0:SEQ], ACT.Copy).then_inc(ybhi_done, 1)

            def mean_hi(g):
                act.wait_ge(mean_done, g + 1)
                act.activation(cols(b_hi, g), ev[:, 2, 0:TOK], ACT.Copy).then_inc(mhi_done, 1)

            def group_hi(g):
                act.wait_ge(full, N_GRP + g + 1)
                act.activation(halves(cols(a_hi, PAIRS + g)), result(N_GRP + g), ACT.Copy,
                               scale=pscale[:, g:g + 1]).then_inc(ghi_done, 1)

            mean_hi(0)
            act.wait_ge(c_done, HEADS + 1)
            act.activation(work_s, zs_ps, ACT.Exp).then_inc(act_own, 1)
            act.activation(work_s2, zs2_ps, ACT.Exp).then_inc(prob_done, 1)
            mean_hi(1)
            group_hi(0)
            mean_hi(2)
            group_hi(1)
            mean_hi(3)
            group_hi(2)
            group_hi(3)

            def sigmoid(m):
                act.activation(gates[:, m, :], gates[:, m, :], ACT.Sigmoid,
                               bias=bgate[:, m:m + 1]).then_inc(sig_done, 1)

            sigmoid(0)
            sigmoid(KT)
            act.wait_ge(y_done, HEADS + 2)
            act.activation(av[:, :, SEQ:TOK], ysb[:, :, SEQ:TOK], ACT.Copy).then_inc(ybhi_done, 1)
            for m in range(KT):
                if m + 1 < KT:
                    sigmoid(m + 1)
                    sigmoid(KT + m + 1)
                split(T_MIX + m + AHEAD)
                act.wait_ge(mix_done, m + 1)
                act.activation(cols(b_hi, m), gates[:, m, :], ACT.Copy).then_inc(bhi_done, 1)
            act.wait_ge(mix_done, KT)
            act.wait_ge(blo_done, KT)
            act.dma_start(p_raw, p_t).then_inc(ple_in, 16)
            act.dma_start(wp_raw, w_ple).then_inc(ple_in, 16)
            for m in range(KT):
                split(T_OUT + m + AHEAD)
                act.wait_ge(taken, N_OUT + m + 1)
                scaled_input(m, g_mlp, KT)
            act.wait_ge(taken, N_STAT1 + 1)
            act.activation(ev[:, 1, 0:TOK], var, ACT.Sqrt).then_inc(root_done, 1)

            def mlp(c, last):
                for j in range(KT):
                    split(T_MLP + j + AHEAD, c, MLP_PER, N_MLP + j)
                    act.wait_ge(h_done, c * KT + (j + 1))
                    act.activation(cols(b_hi, j), work[:, (j % 2) * TOK:(j % 2 + 1) * TOK],
                                   ACT.Copy).then_inc(hhi_done, 1)
                for m in range(KT):
                    split(T_MLP + KT + m + AHEAD, c, MLP_PER, N_MLP + KT + m)
                    if last:
                        act.wait_ge(taken, N_STAT2 - KT + m + 1)
                        scaled_input(m, g_ple, 2 * KT)

            with act.Fori(0, CHUNKS - 1) as c:
                mlp(c, False)
            mlp(CHUNKS - 1, True)
            act.wait_ge(ple_in, 32)
            act.activation(b_hi[:, pr_of:pr_of + 2 * TOK].rearrange("p (k t) -> p k t", k=2), p_raw,
                           ACT.Copy).then_inc(pt_done, 1)
            act.activation(b_hi[:, wp_of:wp_of + 4 * SEQ].rearrange("p (k t) -> p k t", k=4), wp_raw,
                           ACT.Copy).then_inc(pt_done, 1)
            act.wait_ge(taken, N_STAT2 + 1)
            act.activation(ev[:, 1, 0:TOK], var, ACT.Sqrt).then_inc(root_done, 1)
            for m in range(KT):
                if T_PLE + m + AHEAD < N_TILES:
                    split(T_PLE + m + AHEAD)
                act.wait_ge(taken, N_PLE + 2 * m + 1)
                act.activation(gates[:, KT + m, :], gates[:, KT + m, :], ACT.Sigmoid).then_inc(psig_done, 1)
                act.wait_ge(res_done, m + 1)
                if m >= 2:
                    act.wait_ge(sq_added, 3 * KT + m - 1)
                act.activation(ev[:, 1 + m % 2, 0:TOK], xt[:, m, :], ACT.Square).then_inc(sq_done, 1)
            act.wait_ge(taken, N_STAT3 + 1)
            act.activation(ev[:, 1, 0:TOK], var, ACT.Sqrt).then_inc(root_done, 1)
            act.wait_ge(taken, T_MIX)
            act.dma_start(pool_t[0, :, :, :], upad[:, :, U_STATE - STATE:U_STATE]).then_inc(pool_out, 16)
            act.dma_start(pool_t[1, :, :, :], upad[:, :, PADW - STATE:PADW]).then_inc(pool_out, 16)
            act.wait_ge(pool_out, 32)
            for s in kv_out:
                act.wait_ge(s, 16 * PAIRS)

        @block.tensor
        def _(pe):
            def product(out, hi, lo, rhi, rlo, first, last, check=True):
                pe.matmul(out, hi, rhi, start=first, stop=False, skip_group_check=True)
                pe.matmul(out, hi, rlo, start=False, stop=False, skip_group_check=True)
                return pe.matmul(out, lo, rhi, start=False, stop=last, skip_group_check=True)

            def take(n, i=0, per=0):
                before = result_before(n) if isinstance(i, int) and i == 0 else n - 2
                if before is not None:
                    pe.wait_ge(taken, before + 1 + i * per)

            def dense(n, s, ks, acts, ready=None, inc=True, kofs=0):
                base = result(n)
                for q, k in enumerate(ks):
                    if ready is not None:
                        pe.wait_ge(*ready(k))
                    hi, lo = acts
                    for h in range(2):
                        pe.matmul(base[:, h, :], w_hi[:, s, k, :], cols(hi, k - kofs, h * HALF, (h + 1) * HALF),
                                  start=(q == 0), stop=False, skip_group_check=True)
                    for h in range(2):
                        pe.matmul(base[:, h, :], w_hi[:, s, k, :], cols(lo, k - kofs, h * HALF, (h + 1) * HALF),
                                  start=False, stop=False, skip_group_check=True)
                    for h in range(2):
                        mm = pe.matmul(base[:, h, :], w_lo[:, s, k, :],
                                       cols(hi, k - kofs, h * HALF, (h + 1) * HALF),
                                       start=False, stop=(q == len(ks) - 1), skip_group_check=True)
                return mm

            def weights(t, i=0, per=0):
                pe.wait_ge(wlo_done, t + 1 + i * per)

            A = (a_hi, a_lo)
            B = (b_hi, b_lo)

            def tile(j, i, ready=None):
                weights(j, i, S1_PER)
                take(j, i, S1_PER)
                dense(j, j % W_RING, range(KT), A, ready).then_inc(full, 1)

            def stats(n):
                out = psum[:, 4:6, 0:HALF] if n is None else result(n)
                for h in range(2):
                    mm = pe.matmul(out[:, h, :], negone[:, :].bitcast(F32), acc[:, h * HALF:(h + 1) * HALF],
                                   start=True, stop=True)
                return mm

            def scores(hh, i):
                r = slice(DH * hh, DH * hh + DH)
                if hh == 0:
                    pe.wait_ge(qklo_done, 2 * i + 2)
                for b in range(QB):
                    z = z_ps[:, Z_OFF[b]:Z_OFF[b] + Z_LEN[b]]
                    keys = slice(KOF + P * b, KOF + P * (b + 1))
                    qs = slice(QOF + P * b, QOF + SEQ)
                    mm = product(z, b_hi[r, keys], b_lo[r, keys], b_hi[r, qs], b_lo[r, qs], b != 3, b != 1)
                mm.then_inc(z_done, 1)

            def sums(hh, i):
                g = 2 * i + hh
                pe.wait_ge(slo_done, g + 1)
                for b in range(QB):
                    for c in range(b, QB):
                        lhs = negtri if c == b else negone
                        z = z_ps[:, Z_OFF[b] + P * (c - b):Z_OFF[b] + Z_LEN[b]]
                        for part in (b_hi, b_lo):
                            mm = pe.matmul(z, lhs[:, :], part[:, SOF + Z_OFF[c]:SOF + Z_OFF[c] + Z_LEN[c]],
                                           start=False, stop=(c == QB - 1), skip_group_check=True)
                mm.then_inc(c_done, 1)

            def outputs(hh, i):
                g = 2 * i + hh
                pe.wait_ge(plo_done, g + 1)
                if hh == 0:
                    pe.wait_ge(vlo_done, i + 1)
                else:
                    pe.wait_ge(y_done, g)
                for b in range(QB):
                    vs = slice(VOF + P * b, VOF + P * (b + 1))
                    ps = slice(SOF + Z_OFF[b], SOF + Z_OFF[b] + Z_LEN[b])
                    mm = product(o_ps[:, P * b:SEQ], b_hi[:, vs], b_lo[:, vs], b_hi[:, ps], b_lo[:, ps],
                                 b == 0, b == QB - 1)
                mm.then_inc(o_done, 1)

            def v_rows(i):
                pe.wait_ge(taken, 3 + i * S1_PER)
                if not (isinstance(i, int) and i == 0):
                    pe.wait_ge(y_done, 2 * i)
                for b in range(QB):
                    mm = pe.transpose(o_ps[:, P * b:P * (b + 1)], ev[:, 2, P * b:P * (b + 1)], ident[:, :])
                mm.then_inc(vt_done, 1)

            def pair(i):
                first = isinstance(i, int) and i == 0
                ready = (lambda k: (xlo_done, k + 1)) if first else None
                tile(0, i, ready)
                if first:
                    pe.wait_ge(const_made, N_CONST)
                    pe.wait_ge(sq_added, KT)
                    stats(None).then_inc(stat0, 1)
                else:
                    outputs(1, i - 1)
                tile(1, i)
                tile(2, i)
                if first:
                    pe.wait_ge(var_done, 1)
                scores(0, i)
                v_rows(i)
                tile(3, i)
                tile(4, i)
                sums(0, i)
                tile(5, i)
                outputs(0, i)
                scores(1, i)
                tile(6, i)
                tile(7, i)
                sums(1, i)

            pair(0)
            with pe.Fori(1, PAIRS) as i:
                pair(i)
            outputs(1, PAIRS - 1)

            pe.wait_ge(past_in, 32)
            for b in range(2):
                for p in range(PAIRS):
                    pe.matmul(zs_ps[:, b * ZS + p * 2 * DEC:b * ZS + (p + 1) * 2 * DEC],
                              ckt[:, p, P * b:P * (b + 1)], qbd[:, p, :],
                              start=(b == 0 and p == 0), stop=False, skip_group_check=True)
            for p in range(PAIRS):
                mm = pe.matmul(zs2_ps[:, p * 2 * DEC:(p + 1) * 2 * DEC], kst[:, p, :], qbd[:, p, :],
                               start=(p == 0), stop=False, skip_group_check=True)
            mm.then_inc(z_done, 1)
            take(N_VS)
            for p in range(PAIRS):
                mm = pe.transpose(psum[0:DEC, 2 * result_slot(N_VS), P * p:P * (p + 1)], vst[:, p, :], ident[:, :])
            mm.then_inc(full, 1)

            def group(g):
                n = N_GRP + g
                take(n)
                if g == 0:
                    pe.wait_ge(glo_done, 1)
                pe.wait_ge(mlo_done, g + 1)
                wg = slice(GOF + g * P, GOF + (g + 1) * P)
                for h in range(2):
                    c = slice(g * TOK + h * HALF, g * TOK + (h + 1) * HALF)
                    mm = product(result(n)[:, h, :], b_hi[:, wg], b_lo[:, wg], b_hi[:, c], b_lo[:, c], True, True)
                mm.then_inc(full, 1)

            pe.wait_ge(spm_done, HEADS * QB + 1)
            tri, one = negtri[:, :].bitcast(F32), negone[:, :].bitcast(F32)
            for b in range(2):
                z = zs_ps[:, b * ZS:(b + 1) * ZS]
                pe.matmul(z, tri, work[:, b * ZS:(b + 1) * ZS], start=False, stop=False, skip_group_check=True)
                if b == 0:
                    pe.matmul(z, one, work[:, ZS:2 * ZS], start=False, stop=False, skip_group_check=True)
                pe.matmul(z, one[0:DEC, :], work_s2, start=False, stop=True, skip_group_check=True)
            pe.matmul(zs2_ps, tri[0:DEC, 0:DEC], work_s2, start=False, stop=True,
                      skip_group_check=True).then_inc(c_done, 1)
            group(0)
            group(1)
            pe.wait_ge(pm_done, HEADS * QB + 1)
            pe.wait_ge(taken, N_VS + 1)
            for p in range(PAIRS):
                o = os_ps[:, p * 2 * DEC:(p + 1) * 2 * DEC]
                q = slice(p * 2 * DEC, (p + 1) * 2 * DEC)
                for b in range(2):
                    pe.matmul(o, cvn[:, b, P * p:P * (p + 1)], work[:, b * ZS:(b + 1) * ZS][:, q],
                              start=(b == 0), stop=False, skip_group_check=True)
                mm = pe.matmul(o, vsn[:, P * p:P * (p + 1)], work_s2[:, q], start=False, stop=True,
                               skip_group_check=True)
            mm.then_inc(o_done, 1)
            group(2)
            group(3)

            for m in range(KT):
                t, n = T_MIX + m, N_MIX + 2 * m
                weights(t)
                take(n)
                if m == 0:
                    pe.wait_ge(taken, N_GRP + GROUPS)
                dense(n, t % W_RING, range(PAIRS, KT), A).then_inc(full, 1)
                if m == 0:
                    pe.wait_ge(yblo_done, 2)
                if result_before(n + 1) is not None:
                    pe.wait_ge(taken, result_before(n + 1) + 1)
                dense(n + 1, t % W_RING, range(PAIRS), A).then_inc(full, 1)
            for m in range(KT):
                t, n = T_OUT + m, N_OUT + m
                weights(t)
                take(n)
                dense(n, t % W_RING, range(KT), B,
                      (lambda k: (blo_done, k + 1)) if m == 0 else None).then_inc(full, 1)
            take(N_STAT1)
            pe.wait_ge(sq_added, 2 * KT)
            stats(N_STAT1).then_inc(full, 1)

            def mlp(c):
                for j in range(MLP_PER):
                    up = j < KT
                    t, n = T_MLP + j, N_MLP + j
                    weights(t, c, MLP_PER)
                    pe.wait_ge(taken, n - 3 + c * MLP_PER)
                    if up and j == 0:
                        pe.wait_ge(xlo_done, 2 * KT)
                    ready = (lambda k: (hlo_done, c * KT + (k + 1))) if j == KT else None
                    dense(n, t % W_RING, range(KT), A if up else B, ready).then_inc(full, 1)

            with pe.Fori(0, CHUNKS - 1) as c:
                mlp(c)
            mlp(CHUNKS - 1)
            take(N_STAT2)
            pe.wait_ge(sq_added, 3 * KT)
            stats(N_STAT2).then_inc(full, 1)
            for m in range(KT):
                t, n = T_PLE + m, N_PLE + 2 * m
                weights(t)
                take(n)
                dense(n, t % W_RING, range(KT), A,
                      (lambda k: (xlo_done, 2 * KT + k + 1)) if m == 0 else None).then_inc(full, 1)
                take(n + 1)
                if m == 0:
                    pe.wait_ge(ptlo_done, 2)
                for k in range(PLE // P):
                    wsl = slice(wp_of + k * D_MODEL + m * P, wp_of + k * D_MODEL + (m + 1) * P)
                    for h in range(2):
                        c = slice(pr_of + k * TOK + h * HALF, pr_of + k * TOK + (h + 1) * HALF)
                        mm = product(result(n + 1)[:, h, :], b_hi[:, wsl], b_lo[:, wsl], b_hi[:, c], b_lo[:, c],
                                     k == 0, k == 1)
                mm.then_inc(full, 1)
            take(N_STAT3)
            pe.wait_ge(sq_added, 4 * KT)
            stats(N_STAT3).then_inc(full, 1)

        @block.vector
        def _(dve):
            own = [0]

            def link(ins):
                own[0] += 1
                ins.then_inc(dve_own, 1)
                dve.wait_ge(dve_own, own[0])

            def split(t, i=0, per=0):
                s = t % W_RING
                dve.wait_ge(whi_done, t + 1 + i * per)
                dve.tensor_tensor(w_lo[:, s, :, :].rearrange("p k c -> p (k c)"), raw[:, t % RAW_RING, :],
                                  w_hi[:, s, :, :].rearrange("p k c -> p (k c)"), ALU.subtract).then_inc(wlo_done, 1)

            def scaled_input(k, g, n0):
                dve.wait_ge(xhi_done, n0 + k + 1)
                dve.scalar_tensor_tensor(out=cols(a_lo, k), in0=xt[:, k, :], scalar=g[:, k:k + 1],
                                         in1=cols(a_hi, k), op0=ALU.mult, op1=ALU.subtract).then_inc(xlo_done, 1)
                add_square(k, n0)

            def add_square(k, n0):
                dve.wait_ge(sq_done, n0 + k + 1)
                e = ev[:, 1 + k % 2, 0:TOK]
                if k == 0:
                    dve.tensor_copy(acc, e).then_inc(sq_added, 1)
                else:
                    dve.wait_ge(sq_added, n0 + k)
                    dve.tensor_tensor(acc, acc, e, ALU.add).then_inc(sq_added, 1)

            def embeddings_lo():
                dve.wait_ge(pt_done, 2)
                dve.tensor_tensor(b_lo[:, pr_of:pr_of + 2 * TOK].rearrange("p (k t) -> p k t", k=2), p_raw,
                                  b_hi[:, pr_of:pr_of + 2 * TOK].rearrange("p (k t) -> p k t", k=2),
                                  ALU.subtract).then_inc(ptlo_done, 1)
                dve.tensor_tensor(b_lo[:, wp_of:wp_of + 4 * SEQ].rearrange("p (k t) -> p k t", k=4), wp_raw,
                                  b_hi[:, wp_of:wp_of + 4 * SEQ].rearrange("p (k t) -> p k t", k=4),
                                  ALU.subtract).then_inc(ptlo_done, 1)

            def inverse_rms(sums, nth, signal, meanwhile=None):
                dve.tensor_scalar(halves(var), sums, -1.0 / D_MODEL, EPS, ALU.mult, ALU.add).then_inc(signal, 1)
                if meanwhile is not None:
                    meanwhile()
                dve.wait_ge(root_done, nth)
                t = ev[:, 2, 0:TOK]
                link(dve.reciprocal(rn[:, :], ev[:, 1, 0:TOK]))
                link(dve.tensor_tensor(t, rn[:, :], rn[:, :], ALU.mult))
                link(dve.tensor_tensor(t, t, var, ALU.mult))
                link(dve.tensor_scalar(t, t, -0.5, 1.5, ALU.mult, ALU.add))
                link(dve.tensor_tensor(rn[:, :], rn[:, :], t, ALU.mult))

            def normed(n, out, i=0, per=0):
                dve.wait_ge(full, n + 1 + i * per)
                return dve.tensor_tensor(halves(out), result(n), halves(rn[:, :]), ALU.mult)

            dve.wait_ge(vec_in, 16)
            dve.wait_ge(const_made, N_CONST)
            for k in range(KT):
                scaled_input(k, g_mix, 0)
                if k < AHEAD:
                    split(k)
            dve.wait_ge(ghi_done, 1)
            dve.tensor_tensor(b_lo[:, GOF:GOF + GROUPS * P], ev[:, 0, 0:GROUPS * P],
                              b_hi[:, GOF:GOF + GROUPS * P], ALU.subtract).then_inc(glo_done, 1)
            dve.wait_ge(stat0, 1)
            inverse_rms(psum[:, 4:6, 0:HALF], 1, var_done)

            def stick(hh, i):
                g = 2 * i + hh
                dve.wait_ge(ln_done, g + 1)
                dve.scalar_tensor_tensor(out=work[:, :], in0=z_ps, scalar=0.0, in1=work[:, :],
                                         op0=ALU.max, op1=ALU.add).then_inc(sp_done, 1)

            def stick_lo(hh, i):
                dve.wait_ge(shi_done, 2 * i + hh + 1)
                dve.tensor_tensor(b_lo[:, SOF:SOF + Z_COLS], work[:, :], b_hi[:, SOF:SOF + Z_COLS],
                                  ALU.subtract).then_inc(slo_done, 1)

            def prob_lo(hh, i):
                dve.wait_ge(phi_done, 2 * i + hh + 1)
                dve.tensor_tensor(b_lo[:, SOF:SOF + Z_COLS], work[:, :], b_hi[:, SOF:SOF + Z_COLS],
                                  ALU.subtract).then_inc(plo_done, 1)

            def head_out(hh, i):
                r = slice(DH * hh, DH * hh + DH)
                dve.wait_ge(o_done, 2 * i + hh + 1)
                dve.tensor_copy(ysb[r, i, 0:SEQ], o_ps[r, :]).then_inc(y_done, 1)

            def gate(jj, i):
                j = 4 + jj
                dve.wait_ge(full, j + 1 + i * S1_PER)
                dve.tensor_tensor(halves(gates[:, 4 * i + jj, :]), result(j), halves(rn[:, :]), ALU.mult)\
                   .then_inc(taken, 1)

            def pair(i):
                first = isinstance(i, int) and i == 0
                q, k, v = (ev[:, n, 0:TOK] for n in range(3))
                split(AHEAD + 0, i, S1_PER)
                if not first:
                    prob_lo(1, i - 1)
                dve.wait_ge(full, 1 + i * S1_PER)
                dve.scalar_tensor_tensor(out=halves(q), in0=result(0), scalar=DH ** -0.5, in1=halves(rn[:, :]),
                                         op0=ALU.mult, op1=ALU.mult).then_inc(taken, 1)
                dve.wait_ge(taken, 1 + i * S1_PER)
                for h in range(2):
                    r = slice(DH * h, DH * (h + 1))
                    dve.tensor_copy(qbd[r, i, DEC * h:DEC * (h + 1)], q[r, SEQ:TOK])
                dve.wait_ge(qkhi_done, 2 * i + 1)
                dve.tensor_tensor(b_lo[:, QOF:QOF + TOK], q, b_hi[:, QOF:QOF + TOK], ALU.subtract)\
                   .then_inc(qklo_done, 1)
                if not first:
                    head_out(1, i - 1)
                split(AHEAD + 1, i, S1_PER)
                if not first:
                    dve.wait_ge(kv_out[0], 16 * i)
                normed(1, k, i, S1_PER).then_inc(taken, 1)
                dve.wait_ge(taken, 2 + i * S1_PER)
                dve.tensor_copy(kst[:, i, :], k[:, SEQ:TOK])
                dve.wait_ge(qkhi_done, 2 * i + 2)
                dve.tensor_tensor(b_lo[:, KOF:KOF + TOK], k, b_hi[:, KOF:KOF + TOK], ALU.subtract)\
                   .then_inc(qklo_done, 1)
                split(AHEAD + 2, i, S1_PER)
                if not first:
                    dve.wait_ge(kv_out[1], 16 * i)
                normed(2, v, i, S1_PER).then_inc(taken, 1)
                dve.wait_ge(taken, 3 + i * S1_PER)
                dve.tensor_copy(vst[:, i, :], v[:, SEQ:TOK])
                dve.wait_ge(vhi_done, i + 1)
                dve.tensor_tensor(b_lo[:, VOF:VOF + SEQ], o_ps, b_hi[:, VOF:VOF + SEQ], ALU.subtract)\
                   .then_inc(vlo_done, 1)
                stick(0, i)
                split(AHEAD + 3, i, S1_PER)
                dve.wait_ge(full, 4 + i * S1_PER)
                u = upad[:, i, :]
                dve.tensor_tensor(u[:, U_PROMPT:U_PROMPT + HALF], result(3)[:, 0, :], rn[:, 0:HALF], ALU.mult)
                dve.tensor_tensor(u[:, U_PROMPT + HALF:U_STATE], result(3)[:, 1, 0:SEQ - HALF],
                                  rn[:, HALF:SEQ], ALU.mult)
                dve.tensor_tensor(u[:, U_SAMPLE:PADW], result(3)[:, 1, SEQ - HALF:HALF],
                                  rn[:, SEQ:TOK], ALU.mult).then_inc(taken, 1)
                stick_lo(0, i)
                split(AHEAD + 4, i, S1_PER)
                gate(0, i)
                split(AHEAD + 5, i, S1_PER)
                prob_lo(0, i)
                gate(1, i)
                head_out(0, i)
                split(AHEAD + 6, i, S1_PER)
                stick(1, i)
                gate(2, i)
                stick_lo(1, i)
                split(AHEAD + 7, i, S1_PER)
                gate(3, i)

            pair(0)
            with dve.Fori(1, PAIRS) as i:
                pair(i)
            prob_lo(1, PAIRS - 1)
            head_out(1, PAIRS - 1)
            dve.wait_ge(full, N_VS + 1)
            dve.tensor_copy(vsn, psum[0:DEC, 2 * result_slot(N_VS), :]).then_inc(taken, 1)
            dve.wait_ge(ln_done, HEADS + 1)
            dve.scalar_tensor_tensor(out=work_s, in0=zs_ps, scalar=0.0, in1=work_s, op0=ALU.max, op1=ALU.add)
            dve.scalar_tensor_tensor(out=work_s2, in0=zs2_ps, scalar=0.0, in1=work_s2,
                                     op0=ALU.max, op1=ALU.add).then_inc(sp_done, 1)
            for s in kv_out:
                dve.wait_ge(s, 16 * PAIRS)
            dve.wait_ge(state_in, 16)

            def window_mean(g):
                w, u = WINDOWS[g], upad[:, g, :]
                src, lo, reach = u, 0, 1
                for level in range(w.bit_length() - 1):
                    dst = ev[:, level % 2, :]
                    link(dve.tensor_tensor(dst[:, lo + reach:PADW], src[:, lo + reach:PADW],
                                           src[:, lo:PADW - reach], ALU.add))
                    src, lo, reach = dst, lo + reach, 2 * reach
                early = src[:, U_PROMPT:U_PROMPT + w]
                link(dve.scalar_tensor_tensor(out=early, in0=early, scalar=float(w), in1=invc[:, 0:w],
                                              op0=ALU.mult, op1=ALU.mult))
                if g > 0:
                    dve.wait_ge(mlo_done, g)
                for a, n, d in ((U_PROMPT, SEQ, 0), (U_SAMPLE, DEC, SEQ)):
                    ins = dve.scalar_tensor_tensor(out=ev[:, 2, d:d + n], in0=src[:, a:a + n], scalar=1.0 / w,
                                                   in1=u[:, a:a + n], op0=ALU.mult, op1=ALU.subtract)
                ins.then_inc(mean_done, 1)

            def mean_lo(g):
                dve.wait_ge(mhi_done, g + 1)
                dve.tensor_tensor(cols(b_lo, g), ev[:, 2, 0:TOK], cols(b_hi, g), ALU.subtract)\
                   .then_inc(mlo_done, 1)

            def group_lo(g):
                dve.wait_ge(ghi_done, g + 2)
                dve.scalar_tensor_tensor(out=halves(cols(a_lo, PAIRS + g)), in0=result(N_GRP + g),
                                         scalar=pscale[:, g:g + 1], in1=halves(cols(a_hi, PAIRS + g)),
                                         op0=ALU.mult, op1=ALU.subtract).then_inc(taken, 1)

            ah = a_hi[:, 0:PAIRS * TOK].rearrange("p (k t) -> p k t", k=PAIRS)
            al = a_lo[:, 0:PAIRS * TOK].rearrange("p (k t) -> p k t", k=PAIRS)

            def heads_lo(nth, c):
                dve.wait_ge(ybhi_done, nth)
                dve.tensor_tensor(al[:, :, c], ysb[:, :, c], ah[:, :, c], ALU.subtract).then_inc(yblo_done, 1)

            window_mean(0)
            mean_lo(0)
            heads_lo(1, slice(0, SEQ))
            window_mean(1)
            mean_lo(1)
            group_lo(0)
            window_mean(2)
            mean_lo(2)
            group_lo(1)
            dve.wait_ge(o_done, HEADS + 1)
            for h in range(2):
                r = slice(DH * h, DH * (h + 1))
                o = os_ps.rearrange("p (k q) -> p k q", k=PAIRS)
                dve.tensor_copy(ysb[r, :, SEQ:TOK], o[r, :, DEC * h:DEC * (h + 1)]).then_inc(y_done, 1)
            window_mean(3)
            mean_lo(3)
            group_lo(2)
            heads_lo(2, slice(SEQ, TOK))
            group_lo(3)

            for m in range(KT):
                n = N_MIX + 2 * m
                split(T_MIX + m + AHEAD)
                for d, g in enumerate((m, KT + m)):
                    dve.wait_ge(sig_done, 2 * m + d + 1)
                    dve.wait_ge(full, n + d + 1)
                    dve.tensor_tensor(halves(gates[:, g, :]), result(n + d), halves(gates[:, g, :]), ALU.mult)\
                       .then_inc(taken, 1)
                dve.wait_ge(taken, n + 2)
                dve.tensor_tensor(gates[:, m, :], gates[:, m, :], gates[:, KT + m, :], ALU.add)\
                   .then_inc(mix_done, 1)
                dve.wait_ge(bhi_done, m + 1)
                dve.tensor_tensor(cols(b_lo, m), gates[:, m, :], cols(b_hi, m), ALU.subtract)\
                   .then_inc(blo_done, 1)

            def add_residual(n, m, i=0, per=0):
                dve.wait_ge(full, n + 1 + i * per)
                dve.tensor_tensor(halves(xt[:, m, :]), result(n), halves(xt[:, m, :]), ALU.add).then_inc(taken, 1)

            for m in range(KT):
                split(T_OUT + m + AHEAD)
                add_residual(N_OUT + m, m)
                scaled_input(m, g_mlp, KT)
            dve.wait_ge(full, N_STAT1 + 1)
            inverse_rms(result(N_STAT1), 2, taken)

            def mlp(c, last):
                for j in range(KT):
                    split(T_MLP + j + AHEAD, c, MLP_PER)
                    n, h = N_MLP + j, work[:, (j % 2) * TOK:(j % 2 + 1) * TOK]
                    if j >= 2:
                        dve.wait_ge(hlo_done, c * KT + (j - 1))
                    normed(n, h, c, MLP_PER).then_inc(taken, 1)
                    dve.wait_ge(taken, n + 1 + c * MLP_PER)
                    dve.scalar_tensor_tensor(out=h, in0=h, scalar=0.0, in1=h, op0=ALU.max, op1=ALU.mult)\
                       .then_inc(h_done, 1)
                    dve.wait_ge(hhi_done, c * KT + (j + 1))
                    dve.tensor_tensor(cols(b_lo, j), h, cols(b_hi, j), ALU.subtract).then_inc(hlo_done, 1)
                for m in range(KT):
                    split(T_MLP + KT + m + AHEAD, c, MLP_PER)
                    add_residual(N_MLP + KT + m, m, c, MLP_PER)
                    if last:
                        scaled_input(m, g_ple, 2 * KT)

            with dve.Fori(0, CHUNKS - 1) as c:
                mlp(c, False)
            mlp(CHUNKS - 1, True)
            dve.wait_ge(full, N_STAT2 + 1)
            inverse_rms(result(N_STAT2), 3, taken, embeddings_lo)
            for m in range(KT):
                n, s = N_PLE + 2 * m, gates[:, KT + m, :]
                if T_PLE + m + AHEAD < N_TILES:
                    split(T_PLE + m + AHEAD)
                normed(n, s).then_inc(taken, 1)
                dve.wait_ge(psig_done, m + 1)
                dve.wait_ge(full, n + 2)
                dve.tensor_tensor(halves(s), result(n + 1), halves(s), ALU.mult).then_inc(taken, 1)
                dve.wait_ge(taken, n + 2)
                dve.tensor_tensor(xt[:, m, :], xt[:, m, :], s, ALU.add).then_inc(res_done, 1)
                add_square(m, 3 * KT)
            dve.wait_ge(full, N_STAT3 + 1)
            inverse_rms(result(N_STAT3), 4, taken)
            for m in range(KT):
                dve.scalar_tensor_tensor(out=xt[:, m, :], in0=xt[:, m, :], scalar=g_fin[:, m:m + 1],
                                         in1=rn[:, :], op0=ALU.mult, op1=ALU.mult).then_inc(fin_done, 1)


_SHAPES = [("y_t", (KT, P, TOK)), ("k_t", (PAIRS, P, TOK)), ("v_t", (PAIRS, P, TOK)),
           ("pool_t", (2, P, GROUPS, STATE))]


def kernel(x_prompt, x_sample, cache_k, cache_v, state_pool, p_prompt, p_sample,
           g_mix, w_in, b_gate, w_pool_grp, pool_scale, w_pool_up, w_sb_up, w_out,
           g_mlp, w_up, w_down, g_ple, w_ple_gate, w_ple_proj, g_final):
    import concourse.bacc as bacc
    from concourse.bass_utils import run_bass_kernel_spmd

    def rows(a):
        return np.ascontiguousarray(a)

    def column_tiles(w, starts):
        return [w[:, c:c + P].reshape(KT, P, P).transpose(1, 0, 2).reshape(P, KT * P) for c in starts]

    def features_first(prompt, sample):
        return np.concatenate([prompt, sample], axis=0).T

    def per_partition(v):
        return v.reshape(-1, P).T

    (x_prompt, x_sample, cache_k, cache_v, state_pool, p_prompt, p_sample, g_mix, w_in, b_gate, w_pool_grp,
     pool_scale, w_pool_up, w_sb_up, w_out, g_mlp, w_up, w_down, g_ple, w_ple_gate, w_ple_proj, g_final) = (
        np.asarray(a) for a in (x_prompt, x_sample, cache_k, cache_v, state_pool, p_prompt, p_sample, g_mix,
                                w_in, b_gate, w_pool_grp, pool_scale, w_pool_up, w_sb_up, w_out, g_mlp, w_up,
                                w_down, g_ple, w_ple_gate, w_ple_proj, g_final))
    W = HEADS * DH
    tiles = []
    for p in range(PAIRS):
        starts = [W + P * p, 2 * W + P * p, 3 * W + P * p, P * p] + [4 * W + P * (4 * p + j) for j in range(4)]
        tiles += column_tiles(w_in[0], starts)
    every = [P * m for m in range(KT)]
    tiles += column_tiles(np.concatenate([w_sb_up[0], w_pool_up[0]], axis=0), every)
    tiles += column_tiles(w_out[0], every)
    for c in range(CHUNKS):
        tiles += column_tiles(w_up[0], [D_MODEL * c + a for a in every])
        tiles += column_tiles(w_down[0, D_MODEL * c:D_MODEL * (c + 1)], every)
    tiles += column_tiles(w_ple_gate[0], every)
    arrays = {
        "w_tiles": np.stack(tiles),
        "x_t": rows(features_first(x_prompt[0], x_sample[0]).reshape(KT, P, TOK)),
        "p_t": rows(features_first(p_prompt[0, 0], p_sample[0, 0]).reshape(PLE // P, P, TOK).transpose(1, 0, 2)),
        "ck_t": rows(cache_k[0, 0].reshape(PAST, PAIRS, P).transpose(2, 1, 0)),
        "cv": rows(cache_v[0, 0].reshape(PAST // P, P, W).transpose(1, 0, 2)),
        "state_t": rows(state_pool[0, 0].reshape(STATE, GROUPS, P).transpose(2, 1, 0)),
        "w_grp": rows(w_pool_grp[0].transpose(1, 0, 2).reshape(P, GROUPS * P)),
        "w_ple": rows(w_ple_proj[0].reshape(PLE // P, P, 2, SEQ).transpose(1, 0, 2, 3).reshape(P, 4, SEQ)),
        "vecs": rows(np.concatenate([per_partition(a) for a in (g_mix[0], g_mlp[0], g_ple[0], g_final,
                                                                 b_gate[0], pool_scale[0])], axis=1)),
    }
    nc = bacc.Bacc("TRN2", target_bir_lowering=False, num_devices=1)
    ins = [nc.dram_tensor(n, a.shape, F32, kind="ExternalInput").ap() for n, a in arrays.items()]
    outs = [nc.dram_tensor(n, s, F32, kind="ExternalOutput").ap() for n, s in _SHAPES]
    hybrid_step_kernel(nc, *ins, *outs)
    r = run_bass_kernel_spmd(nc, [arrays], core_ids=[0]).results[0]
    y, k, v, pool = (r[n] for n, _ in _SHAPES)
    y = y.reshape(D_MODEL, TOK).T
    k, v = (a.reshape(W, TOK).T.reshape(TOK, HEADS, DH) for a in (k, v))
    pool = pool.transpose(0, 3, 2, 1).reshape(2, STATE, GROUPS * P)
    return (rows(y[None, :SEQ]), rows(y[None, SEQ:]), rows(k[None, None, :SEQ]), rows(v[None, None, :SEQ]),
            rows(pool[0][None, None]), rows(k[None, None, SEQ:]), rows(v[None, None, SEQ:]),
            rows(pool[1][None, None]))
```

```python
from contextlib import ExitStack

import numpy as np

import concourse.bass as bass
from concourse import mybir

ALU = mybir.AluOpType
ACT = mybir.ActivationFunctionType
F32 = mybir.dt.float32
F32R = mybir.dt.float32r

P = 128
D_MODEL = 1024
SEQ = 512
DEC = 32
PAST = 256
TOK = SEQ + DEC
HALF = TOK // 2
HEADS = 8
DH = 64
PAIRS = HEADS * DH // P
GROUPS = 4
WINDOWS = (2, 4, 8, 16)
STATE = max(WINDOWS) - 1
D_FF = 4 * D_MODEL
PLE = 256
EPS = 1e-6
KT = D_MODEL // P
QB = SEQ // P

S1_PER = 8
POOL_SQUARES = KT // 2
T_MIX = PAIRS * S1_PER
T_OUT = T_MIX + KT
T_MLP = T_OUT + KT
CHUNKS = D_FF // D_MODEL
MLP_PER = 2 * KT
T_PLE = T_MLP + CHUNKS * MLP_PER
N_TILES = T_PLE + KT
W_RING = 4
RAW_RING = 2
AHEAD = W_RING - 1

N_GRP = T_MIX
N_VS = N_GRP + GROUPS + KT // 2
N_POOL = [N_GRP + GROUPS + m + (m >= KT // 2) for m in range(KT)]
N_ATT = N_GRP + GROUPS + KT + 1
N_OUT = N_ATT + KT
N_STAT1 = N_OUT + KT + 1
N_MLP = N_STAT1
N_STAT2 = N_MLP + CHUNKS * MLP_PER + 1
N_PLE = N_STAT2
N_STAT3 = N_PLE + 2 * KT


def mlp_result(j):
    return N_MLP + j if j else N_STAT1 - 1


def gate_result(m):
    return N_PLE + 2 * m if m else N_STAT2 - 1


Z_OFF = (0, 512, 1024, 896)
Z_LEN = tuple(SEQ - P * b for b in range(QB))
Z_COLS = sum(Z_LEN)
ZS = HEADS * DEC
PADW = STATE + SEQ + STATE + DEC
U_PROMPT = STATE
U_STATE = STATE + SEQ
U_SAMPLE = U_STATE + STATE


LOG_EXP = "natural_log_exp_and_others"
SIGMOID = "sigmoid_and_others"


def result_slot(n):
    return n % 4 if n < 4 or n >= N_ATT else n % 2


def taken_by(n):
    return n + 2 if n in (N_STAT1 - 1, N_STAT2 - 1) else n if n in (N_STAT1, N_STAT2) else n + 1


def result_before(n):
    for m in range(n - 1, -1, -1):
        if result_slot(m) == result_slot(n):
            return m
    return None


def results_by(t):
    if t < 0:
        return None
    if t < T_MIX:
        return t + 1
    if t < T_MIX + KT // 2:
        return N_POOL[2 * (t - T_MIX) + 1] + 1
    if t < T_OUT:
        return N_ATT + 2 * (t - T_MIX - KT // 2) + 2
    if t < T_MLP:
        return N_OUT + (t - T_OUT) + 1
    if t < T_PLE:
        return mlp_result(t - T_MLP) + 1
    return gate_result(t - T_PLE) + 1


def hybrid_step_kernel(nc, w_tiles, x_t, p_t, ck_t, cv, state_t, w_grp, w_ple, vecs,
                       y_t, k_t, v_t, pool_t):
    ctx = ExitStack()
    with ctx:
        def sb(name, shape, dt=F32):
            return ctx.enter_context(nc.sbuf_tensor(name, shape, dt))

        def sem(name):
            return ctx.enter_context(nc.semaphore(name))

        raw = sb("raw", [P, RAW_RING, D_MODEL])
        w_hi = sb("w_hi", [P, W_RING, KT, P], F32R)
        w_lo = sb("w_lo", [P, W_RING, KT, P], F32R)
        a_hi = sb("a_hi", [P, KT * TOK], F32R)
        a_lo = sb("a_lo", [P, KT * TOK], F32R)
        b_hi = sb("b_hi", [P, KT * TOK], F32R)
        b_lo = sb("b_lo", [P, KT * TOK], F32R)
        xt = sb("xt", [P, KT, TOK])
        gates = sb("gates", [P, 2 * KT, TOK])
        rn = sb("rn", [P, TOK])
        ev = sb("ev", [P, 3, 576])
        upad = sb("upad", [P, GROUPS, PADW])
        ysb = sb("ysb", [P, PAIRS, TOK])
        work = sb("work", [P, Z_COLS])
        ckt = sb("ckt", [P, PAIRS, PAST])
        cvn = sb("cvn", [P, PAST // P, HEADS * DH])
        qbd = sb("qbd", [P, PAIRS, 2 * DEC])
        kst = sb("kst", [P, PAIRS, DEC])
        vst = sb("vst", [P, PAIRS, DEC])
        ident = sb("ident", [P, P])
        negtri = sb("negtri", [P, P], F32R)
        negone = sb("negone", [P, P], F32R)
        vec = sb("vec", [P, 4 * KT + 2 * KT + GROUPS])
        invc = sb("invc", [P, STATE + 1])
        mean0 = [sb("mean0_hi", [P, TOK], F32R), sb("mean0_lo", [P, TOK], F32R)]
        psum = ctx.enter_context(nc.psum_tensor("psum", [P, 8, 512], F32))

        g_mix, g_mlp, g_ple, g_fin, bgate, pscale = (
            vec[:, 0:KT], vec[:, KT:2 * KT], vec[:, 2 * KT:3 * KT], vec[:, 3 * KT:4 * KT],
            vec[:, 4 * KT:6 * KT], vec[:, 6 * KT:6 * KT + GROUPS])

        def halves(ap):
            return ap.rearrange("p (a c) -> p a c", a=2)

        def cols(buf, k, lo=0, hi=TOK):
            return buf[:, k * TOK + lo:k * TOK + hi]

        def result(n):
            s = result_slot(n)
            return psum[:, 2 * s:2 * s + 2, 0:HALF]

        def pair_result(j, i):
            return result(j if isinstance(i, int) and i == 0 else S1_PER + j)

        flat = psum[:, 4:7, :].rearrange("p a c -> p (a c)")
        z_ps = flat[:, 0:Z_COLS]
        o_ps = psum[:, 7, :]
        zs_ps = psum[:, 4, :]
        zs2_ps = psum[0:DEC, 5, 0:ZS]
        os_ps = psum[:, 6, 0:ZS]

        QOF, KOF, VOF, SOF, GOF = 0, TOK, 2 * TOK, 2 * TOK + SEQ, KT * TOK - GROUPS * P
        MOF = SOF + Z_COLS
        assert MOF + TOK <= GOF
        gates_flat = gates[:, :, :].rearrange("p k t -> p (k t)")
        window = [gates_flat[:, 2 * KT * TOK - n * PADW:][:, 0:PADW] for n in (1, 2)]

        def mean_part(part, g):
            return mean0[part][:, :] if g == 0 else (b_hi, b_lo)[part][:, (QOF, KOF, MOF)[g - 1]:][:, 0:TOK]

        work_s = work[:, 0:2 * ZS]
        work_s2 = work[0:DEC, 2 * ZS:3 * ZS]
        vsn = work[0:DEC, 3 * ZS:3 * ZS + HEADS * DH]
        acc = work[:, 0:TOK]
        var = work[:, TOK:2 * TOK]
        p_raw = gates[:, 0:2, :]
        wp_raw = gates[:, 2:6, 0:SEQ]
        pr_of, wp_of = 0, 2 * TOK

        taken = sem("taken")
        x_in = [sem(f"x_in{k}") for k in range(KT)]
        vec_in = sem("vec_in")
        grp_in = sem("grp_in")
        past_in = sem("past_in")
        state_in = sem("state_in")
        ple_in = sem("ple_in")
        half_in = [sem("half_in0"), sem("half_in1")]
        half_hi_done = sem("half_hi_done")
        half_lo_done = sem("half_lo_done")
        raw_in = [sem(f"raw_in{s}") for s in range(RAW_RING)]
        whi_done = sem("whi_done")
        wlo_done = sem("wlo_done")
        full = sem("full")
        const_made = sem("const_made")
        base_made = sem("base_made")
        xhi_done = sem("xhi_done")
        xlo_done = sem("xlo_done")
        pool_own = sem("pool_own")
        sq_done = sem("sq_done")
        sq_added = sem("sq_added")
        stat0 = sem("stat0")
        var_done = sem("var_done")
        log_done = sem("log_done")
        root_done = sem("root_done")
        dve_own = sem("dve_own")
        act_own = sem("act_own")
        qkhi_done = sem("qkhi_done")
        qklo_done = sem("qklo_done")
        vt_done = sem("vt_done")
        vhi_done = sem("vhi_done")
        vlo_done = sem("vlo_done")
        kv_out = [sem("k_out"), sem("v_out")]
        z_done = sem("z_done")
        ln_done = sem("ln_done")
        sp_done = sem("sp_done")
        spm_done = sem("spm_done")
        shi_done = sem("shi_done")
        slo_done = sem("slo_done")
        c_done = sem("c_done")
        prob_done = sem("prob_done")
        pm_done = sem("pm_done")
        phi_done = sem("phi_done")
        plo_done = sem("plo_done")
        o_done = sem("o_done")
        y_done = sem("y_done")
        mean_done = sem("mean_done")
        mhi_done = sem("mhi_done")
        mlo_done = sem("mlo_done")
        ghi_done = sem("ghi_done")
        glo_done = sem("glo_done")
        ybhi_done = sem("ybhi_done")
        yblo_done = sem("yblo_done")
        sig_done = sem("sig_done")
        mix_done = sem("mix_done")
        bhi_done = sem("bhi_done")
        blo_done = sem("blo_done")
        res_done = sem("res_done")
        h_done = sem("h_done")
        hhi_done = sem("hhi_done")
        hlo_done = sem("hlo_done")
        pt_done = sem("pt_done")
        ptlo_done = sem("ptlo_done")
        psig_done = sem("psig_done")
        fin_done = sem("fin_done")
        out_done = sem("out_done")
        pool_out = sem("pool_out")

        block = ctx.enter_context(nc.Block())
        N_CONST = STATE + 1 + 5

        @block.sync
        def _(sp):
            first = (("w", 0), ("x", 0), ("x", 1), ("w", 1), ("x", 2), ("x", 3), ("x", 4), ("w", 2), ("x", 5),
                     ("x", 6), ("x", 7))
            for what, n in first:
                if what == "x":
                    sp.dma_start(xt[:, n, :], x_t[n, :, :]).then_inc(x_in[n], 16)
                elif n < 2:
                    part = slice(n * D_MODEL // 2, (n + 1) * D_MODEL // 2)
                    sp.dma_start(raw[:, 0, part], w_tiles[0, :, part]).then_inc(half_in[n], 16)
                else:
                    sp.dma_start(raw[:, 1, :], w_tiles[1, :, :]).then_inc(raw_in[1], 16)
            with sp.Fori(1, N_TILES // RAW_RING) as r:
                for s in range(RAW_RING):
                    sp.wait_ge(wlo_done, r * RAW_RING + (s - RAW_RING + 1))
                    sp.dma_start(raw[:, s, :], w_tiles[r * RAW_RING + s, :, :]).then_inc(raw_in[s], 16)
            for k in range(KT):
                sp.wait_ge(fin_done, k + 1)
                sp.dma_start(y_t[k, :, :], xt[:, k, :]).then_inc(out_done, 16)
            sp.wait_ge(out_done, 16 * KT)

        @block.gpsimd
        def _(pool):
            pool.memset(ident[:, :], 0.0).then_inc(base_made, 1)
            pool.memset(work[:, 0:P], -1.0).then_inc(base_made, 1)
            pool.memset(work[:, P:2 * P], -1.0).then_inc(base_made, 1)
            for n in range(STATE + 1):
                pool.memset(invc[:, n:n + 1], 1.0 / (n + 1)).then_inc(const_made, 1)
            pool.memset(qbd[:, :, :], 0.0).then_inc(const_made, 1)
            pool.memset(upad[:, :, 0:STATE], 0.0).then_inc(const_made, 1)
            pool.wait_ge(base_made, 3)
            pool.affine_select(out=ident[:, :], in_=ident[:, :], compare_op=ALU.not_equal, fill=1.0,
                               base=0, pattern=[[-1, P]], channel_multiplier=1).then_inc(const_made, 1)
            pool.affine_select(out=negtri[:, :], in_=work[:, 0:P], compare_op=ALU.is_ge, fill=0.0,
                               base=0, pattern=[[-1, P]], channel_multiplier=1).then_inc(const_made, 1)
            pool.tensor_copy(negone[:, :], work[:, P:2 * P]).then_inc(const_made, 1)

            pool_own_count = [0]

            def link(ins):
                pool_own_count[0] += 1
                ins.then_inc(pool_own, 1)
                pool.wait_ge(pool_own, pool_own_count[0])

            pool.wait_ge(const_made, N_CONST)
            for k in range(POOL_SQUARES):
                x, e = xt[:, k, :], ev[:, 1 + k % 2, 0:TOK]
                pool.wait_ge(x_in[k], 16)
                if k == 0:
                    pool.tensor_tensor(acc, x, x, ALU.mult).then_inc(sq_added, 1)
                else:
                    link(pool.tensor_tensor(e, x, x, ALU.mult))
                    pool.wait_ge(sq_added, k)
                    pool.tensor_tensor(acc, acc, e, ALU.add).then_inc(sq_added, 1)

            def window_sums(g):
                pool.wait_ge(taken, 4 + g * S1_PER)
                if g == 0:
                    pool.wait_ge(state_in, 16)
                u = upad[:, g, :]
                pool.dma_start(pool_t[0, :, g, :], u[:, U_STATE - STATE:U_STATE]).then_inc(pool_out, 16)
                pool.dma_start(pool_t[1, :, g, :], u[:, PADW - STATE:PADW]).then_inc(pool_out, 16)
                src, lo, reach = u, 0, 1
                for level in range(WINDOWS[g].bit_length() - 1):
                    dst = window[level % 2]
                    link(pool.tensor_tensor(dst[:, lo + reach:PADW], src[:, lo + reach:PADW],
                                            src[:, lo:PADW - reach], ALU.add))
                    src, lo, reach = dst, lo + reach, 2 * reach
                return src

            def window_mean(g, src):
                w, u = WINDOWS[g], upad[:, g, :]
                early = src[:, U_PROMPT:U_PROMPT + w]
                full_sum, mean = src[:, U_PROMPT + w:PADW], src[:, U_PROMPT:PADW]
                pool.tensor_scalar(full_sum, full_sum, 1.0 / w, None, ALU.mult)
                link(pool.tensor_tensor(early, early, invc[:, 0:w], ALU.mult))
                pool.wait_ge(pool_out, 32 * (g + 1))
                pool.tensor_tensor(u[:, U_PROMPT:PADW], mean, u[:, U_PROMPT:PADW], ALU.subtract)\
                    .then_inc(mean_done, 1)

            def mask_diagonals(done):
                for b in range(QB):
                    d = work[:, Z_OFF[b]:Z_OFF[b] + P]
                    pool.affine_select(out=d, in_=d, compare_op=ALU.is_gt, fill=0.0,
                                       base=0, pattern=[[1, P]], channel_multiplier=-1).then_inc(done, 1)

            for g in range(HEADS):
                pool.wait_ge(sp_done, g + 1)
                mask_diagonals(spm_done)
                if g % 2 == 0:
                    sums = window_sums(g // 2)
                if g == HEADS - 2:
                    window_mean(g // 2, sums)
                pool.wait_ge(prob_done, g + 1)
                mask_diagonals(pm_done)
                if g % 2 == 0 and g != HEADS - 2:
                    window_mean(g // 2, sums)
            new = work_s2.rearrange("p (h q) -> p h q", h=HEADS)
            for ready, done in ((sp_done, spm_done), (prob_done, pm_done)):
                pool.wait_ge(ready, HEADS + 1)
                pool.affine_select(out=new, in_=new, compare_op=ALU.is_gt, fill=0.0,
                                   base=0, pattern=[[0, HEADS], [1, DEC]], channel_multiplier=-1).then_inc(done, 1)

        @block.scalar
        def _(act):
            act.dma_start(vec[:, :], vecs).then_inc(vec_in, 16)

            def split(t, i=0, per=0, left=None):
                if left is None:
                    left = results_by(t - W_RING)
                s = t % W_RING
                act.wait_ge(raw_in[t % RAW_RING], 16 * (t // RAW_RING + t % RAW_RING) + i * (16 * per // RAW_RING))
                if left is not None:
                    act.wait_ge(full, left + i * per)
                act.activation(w_hi[:, s, :, :].rearrange("p k c -> p (k c)"), raw[:, t % RAW_RING, :],
                               ACT.Copy).then_inc(whi_done, 1)

            def input_hi(k, g):
                act.activation(cols(a_hi, k), xt[:, k, :], ACT.Copy, scale=g[:, k:k + 1]).then_inc(xhi_done, 1)

            def square(k, n0):
                if k >= 2:
                    act.wait_ge(sq_added, n0 + k - 1)
                act.activation(ev[:, 1 + k % 2, 0:TOK], xt[:, k, :], ACT.Square).then_inc(sq_done, 1)

            def root(nth):
                act.activation(ev[:, 1, 0:TOK], var, ACT.Ln).then_inc(log_done, 1)
                act.wait_ge(log_done, nth)
                act.activation(ev[:, 1, 0:TOK], ev[:, 1, 0:TOK], ACT.Exp, scale=-0.5).then_inc(root_done, 1)

            def tables(name):
                act.preload_act_table_set(name)

            def half(n, done):
                part = slice(n * D_MODEL // 2, (n + 1) * D_MODEL // 2)
                act.wait_ge(half_in[n], 16)
                act.activation(w_hi[:, 0, :, :].rearrange("p k c -> p (k c)")[:, part], raw[:, 0, part],
                               ACT.Copy).then_inc(done, 1)

            tables(LOG_EXP)
            half(0, half_hi_done)
            act.wait_ge(vec_in, 16)
            for k in range(KT):
                act.wait_ge(x_in[k], 16)
                input_hi(k, g_mix)
                if k == 1:
                    half(1, whi_done)
                if k == 4:
                    split(1)
            act.dma_start(ev[:, 0, 0:GROUPS * P], w_grp).then_inc(grp_in, 16)
            act.dma_start(upad[:, :, U_STATE:U_SAMPLE], state_t).then_inc(state_in, 16)
            for k in range(POOL_SQUARES, KT):
                square(k, 0)
                if k == POOL_SQUARES + 1:
                    split(2)
            act.wait_ge(grp_in, 16)
            act.activation(b_hi[:, GOF:GOF + GROUPS * P], ev[:, 0, 0:GROUPS * P], ACT.Copy).then_inc(ghi_done, 1)
            split(3)
            act.wait_ge(var_done, 1)
            root(1)

            def chain(hh, i):
                g = 2 * i + hh
                act.wait_ge(z_done, g + 1)
                act.activation(work[:, :], z_ps, ACT.Abs).then_inc(act_own, 1)
                act.wait_ge(act_own, 2 * g + 1)
                act.activation(work[:, :], work[:, :], ACT.Exp, scale=-1.0).then_inc(act_own, 1)
                act.wait_ge(act_own, 2 * g + 2)
                act.activation(work[:, :], work[:, :], ACT.Ln, bias=1.0).then_inc(ln_done, 1)

            def stick_hi(hh, i):
                g = 2 * i + hh
                act.wait_ge(spm_done, g * QB + QB)
                act.activation(b_hi[:, SOF:SOF + Z_COLS], work[:, :], ACT.Copy).then_inc(shi_done, 1)

            def prob(hh, i):
                g = 2 * i + hh
                act.wait_ge(c_done, g + 1)
                act.activation(work[:, :], z_ps, ACT.Exp).then_inc(prob_done, 1)

            def prob_hi(hh, i):
                g = 2 * i + hh
                act.wait_ge(pm_done, g * QB + QB)
                act.activation(b_hi[:, SOF:SOF + Z_COLS], work[:, :], ACT.Copy).then_inc(phi_done, 1)

            def mean_hi(g):
                act.wait_ge(mean_done, g + 1)
                out = mean_part(0, g)
                act.activation(out[:, 0:SEQ], upad[:, g, U_PROMPT:U_STATE], ACT.Copy)
                act.activation(out[:, SEQ:TOK], upad[:, g, U_SAMPLE:PADW], ACT.Copy).then_inc(mhi_done, 1)

            def sigmoid(m):
                act.activation(gates[:, m, :], gates[:, m, :], ACT.Sigmoid,
                               bias=bgate[:, m:m + 1]).then_inc(sig_done, 1)

            def pair(i):
                first = isinstance(i, int) and i == 0
                last = isinstance(i, int) and i == PAIRS - 1
                if not first:
                    split(AHEAD + 0, i, S1_PER, 0)
                act.wait_ge(taken, 1 + i * S1_PER)
                act.activation(b_hi[:, QOF:QOF + TOK], ev[:, 0, 0:TOK], ACT.Copy).then_inc(qkhi_done, 1)
                split(AHEAD + 1, i, S1_PER, 1)
                act.wait_ge(taken, 2 + i * S1_PER)
                act.activation(b_hi[:, KOF:KOF + TOK], ev[:, 1, 0:TOK], ACT.Copy).then_inc(qkhi_done, 1)
                act.dma_start(k_t[i, :, :], ev[:, 1, 0:TOK]).then_inc(kv_out[0], 16)
                if not first:
                    prob(1, i - 1)
                split(AHEAD + 2, i, S1_PER, 2)
                if not first:
                    prob_hi(1, i - 1)
                chain(0, i)
                split(AHEAD + 3, i, S1_PER, 3)
                stick_hi(0, i)
                act.wait_ge(taken, 3 + i * S1_PER)
                act.dma_start(v_t[i, :, :], ev[:, 2, 0:TOK]).then_inc(kv_out[1], 16)
                act.wait_ge(vt_done, i + 1)
                act.activation(b_hi[:, VOF:VOF + SEQ], o_ps, ACT.Copy).then_inc(vhi_done, 1)
                split(AHEAD + 4, i, S1_PER, 4)
                if last:
                    tables(SIGMOID)
                    for m in range(KT):
                        sigmoid(m)
                    tables(LOG_EXP)
                    mean_hi(0)
                split(AHEAD + 5, i, S1_PER, 5)
                prob(0, i)
                split(AHEAD + 6, i, S1_PER, 6)
                prob_hi(0, i)
                chain(1, i)
                split(AHEAD + 7, i, S1_PER, 7)
                if last:
                    mean_hi(1)
                stick_hi(1, i)
                if last:
                    mean_hi(2)
                    mean_hi(3)

            pair(0)
            act.dma_start(ckt[:, :, :], ck_t).then_inc(past_in, 16)
            act.dma_start(cvn[:, :, :], cv).then_inc(past_in, 16)
            with act.Fori(1, PAIRS - 1) as i:
                pair(i)
            pair(PAIRS - 1)
            def group_hi(g):
                act.wait_ge(full, N_GRP + g + 1)
                act.activation(halves(cols(a_hi, PAIRS + g)), result(N_GRP + g), ACT.Copy,
                               scale=pscale[:, g:g + 1]).then_inc(ghi_done, 1)

            for g in range(GROUPS):
                group_hi(g)
            split(T_MIX + AHEAD)
            split(T_MIX + 1 + AHEAD)
            prob(1, PAIRS - 1)
            prob_hi(1, PAIRS - 1)
            split(T_MIX + 2 + AHEAD)
            act.wait_ge(y_done, HEADS)
            av = a_hi[:, 0:PAIRS * TOK].rearrange("p (k t) -> p k t", k=PAIRS)
            act.activation(av[:, :, 0:SEQ], ysb[:, :, 0:SEQ], ACT.Copy).then_inc(ybhi_done, 1)
            act.wait_ge(z_done, HEADS + 1)
            act.wait_ge(plo_done, HEADS)
            act.activation(work_s, zs_ps, ACT.Abs).then_inc(act_own, 1)
            act.activation(work_s2, zs2_ps, ACT.Abs).then_inc(act_own, 1)
            act.wait_ge(act_own, 2 * HEADS + 2)
            act.activation(work_s, work_s, ACT.Exp, scale=-1.0).then_inc(act_own, 1)
            act.activation(work_s2, work_s2, ACT.Exp, scale=-1.0).then_inc(act_own, 1)
            act.wait_ge(act_own, 2 * HEADS + 4)
            act.activation(work_s, work_s, ACT.Ln, bias=1.0).then_inc(act_own, 1)
            act.activation(work_s2, work_s2, ACT.Ln, bias=1.0).then_inc(ln_done, 1)
            split(T_MIX + 3 + AHEAD)
            act.wait_ge(c_done, HEADS + 1)
            act.activation(work_s, zs_ps, ACT.Exp).then_inc(act_own, 1)
            act.activation(work_s2, zs2_ps, ACT.Exp).then_inc(prob_done, 1)
            tables(SIGMOID)
            act.wait_ge(y_done, HEADS + 2)
            act.activation(av[:, :, SEQ:TOK], ysb[:, :, SEQ:TOK], ACT.Copy).then_inc(ybhi_done, 1)
            act.wait_ge(taken, T_MIX)
            for m in range(KT):
                sigmoid(KT + m)
            for m in range(KT):
                if m % 2 == 0:
                    split(T_MIX + KT // 2 + m // 2 + AHEAD)
                act.wait_ge(mix_done, m + 1)
                act.activation(cols(b_hi, m), gates[:, m, :], ACT.Copy).then_inc(bhi_done, 1)
            tables(LOG_EXP)
            act.wait_ge(blo_done, KT)
            act.dma_start(p_raw, p_t).then_inc(ple_in, 16)
            act.dma_start(wp_raw, w_ple).then_inc(ple_in, 16)
            for m in range(KT):
                split(T_OUT + m + AHEAD)
                act.wait_ge(taken, N_OUT + m + 1)
                input_hi(m, g_mlp)
                square(m, KT)

            def mlp(c, j, last=False):
                split(T_MLP + j + AHEAD, c, MLP_PER, mlp_result(j - 1) + 1 if j else None)
                if isinstance(c, int) and c == 0 and j == 0:
                    act.wait_ge(taken, taken_by(N_STAT1))
                    root(2)
                if j % MLP_PER < KT:
                    k = j % MLP_PER
                    act.wait_ge(h_done, c * KT + (j // MLP_PER * KT + k + 1))
                    act.activation(cols(b_hi, k), work[:, (k % 2) * TOK:(k % 2 + 1) * TOK],
                                   ACT.Copy).then_inc(hhi_done, 1)
                elif last:
                    m = j - KT
                    act.wait_ge(taken, N_MLP + c * MLP_PER + j + 1)
                    input_hi(m, g_ple)
                    square(m, 2 * KT)

            mlp(0, 0)
            with act.Fori(0, CHUNKS - 1) as c:
                for j in range(1, MLP_PER + 1):
                    mlp(c, j)
            for j in range(1, MLP_PER):
                mlp(CHUNKS - 1, j, last=True)
            act.wait_ge(ple_in, 32)
            act.activation(b_hi[:, pr_of:pr_of + 2 * TOK].rearrange("p (k t) -> p k t", k=2), p_raw,
                           ACT.Copy).then_inc(pt_done, 1)
            act.activation(b_hi[:, wp_of:wp_of + 4 * SEQ].rearrange("p (k t) -> p k t", k=4), wp_raw,
                           ACT.Copy).then_inc(pt_done, 1)
            act.wait_ge(taken, taken_by(N_STAT2))
            root(3)
            tables(SIGMOID)
            for m in range(KT):
                if T_PLE + m + AHEAD < N_TILES:
                    split(T_PLE + m + AHEAD)
                act.wait_ge(taken, taken_by(gate_result(m)))
                act.activation(gates[:, KT + m, :], gates[:, KT + m, :], ACT.Sigmoid).then_inc(psig_done, 1)
                if m == KT - 1:
                    tables(LOG_EXP)
                act.wait_ge(res_done, m + 1)
                square(m, 3 * KT)
            act.wait_ge(taken, taken_by(N_STAT3))
            root(4)
            act.wait_ge(pool_out, 32)
            for s in kv_out:
                act.wait_ge(s, 16 * PAIRS)

        @block.tensor
        def _(pe):
            def product(out, hi, lo, rhi, rlo, first, last, check=True):
                pe.matmul(out, hi, rhi, start=first, stop=False, skip_group_check=True)
                pe.matmul(out, hi, rlo, start=False, stop=False, skip_group_check=True)
                return pe.matmul(out, lo, rhi, start=False, stop=last, skip_group_check=True)

            def take(n, i=0, per=0):
                before = result_before(n) if isinstance(i, int) and i == 0 else n - 2
                if before is not None:
                    pe.wait_ge(taken, taken_by(before) + i * per)

            def dense(base, s, ks, acts, ready=None, weights_ready=None):
                for q, (k, wk) in enumerate(ks):
                    if ready is not None:
                        pe.wait_ge(*ready(k))
                    if weights_ready is not None and k % (KT // 2) == 0:
                        pe.wait_ge(*weights_ready(k))
                    hi, lo = acts
                    for h in range(2):
                        pe.matmul(base[:, h, :], w_hi[:, s, wk, :], cols(hi, k, h * HALF, (h + 1) * HALF),
                                  start=(q == 0), stop=False, skip_group_check=True)
                    for h in range(2):
                        pe.matmul(base[:, h, :], w_hi[:, s, wk, :], cols(lo, k, h * HALF, (h + 1) * HALF),
                                  start=False, stop=False, skip_group_check=True)
                    for h in range(2):
                        mm = pe.matmul(base[:, h, :], w_lo[:, s, wk, :],
                                       cols(hi, k, h * HALF, (h + 1) * HALF),
                                       start=False, stop=(q == len(ks) - 1), skip_group_check=True)
                return mm

            def weights(t, i=0, per=0):
                pe.wait_ge(wlo_done, t + 1 + i * per)

            ALL = [(k, k) for k in range(KT)]
            A = (a_hi, a_lo)
            B = (b_hi, b_lo)

            def tile(j, i):
                weights(j, i, S1_PER)
                take(j, i, S1_PER)
                dense(pair_result(j, i), j % W_RING, ALL, A).then_inc(full, 1)

            def stats(n):
                out = psum[:, 6:8, 0:HALF] if n is None else result(n)
                for h in range(2):
                    mm = pe.matmul(out[:, h, :], negone[:, :].bitcast(F32), acc[:, h * HALF:(h + 1) * HALF],
                                   start=True, stop=True)
                return mm

            def scores(hh, i):
                r = slice(DH * hh, DH * hh + DH)
                if hh == 0:
                    pe.wait_ge(qklo_done, 2 * i + 2)
                for b in range(QB):
                    z = z_ps[:, Z_OFF[b]:Z_OFF[b] + Z_LEN[b]]
                    keys = slice(KOF + P * b, KOF + P * (b + 1))
                    qs = slice(QOF + P * b, QOF + SEQ)
                    mm = product(z, b_hi[r, keys], b_lo[r, keys], b_hi[r, qs], b_lo[r, qs], b != 3, b != 1)
                mm.then_inc(z_done, 1)

            def sums(hh, i):
                g = 2 * i + hh
                pe.wait_ge(slo_done, g + 1)
                for b in range(QB):
                    for c in range(b, QB):
                        lhs = negtri if c == b else negone
                        z = z_ps[:, Z_OFF[b] + P * (c - b):Z_OFF[b] + Z_LEN[b]]
                        for part in (b_hi, b_lo):
                            mm = pe.matmul(z, lhs[:, :], part[:, SOF + Z_OFF[c]:SOF + Z_OFF[c] + Z_LEN[c]],
                                           start=False, stop=(c == QB - 1), skip_group_check=True)
                mm.then_inc(c_done, 1)

            def outputs(hh, i):
                g = 2 * i + hh
                pe.wait_ge(plo_done, g + 1)
                if hh == 0:
                    pe.wait_ge(vlo_done, i + 1)
                else:
                    pe.wait_ge(y_done, g)
                for b in range(QB):
                    vs = slice(VOF + P * b, VOF + P * (b + 1))
                    ps = slice(SOF + Z_OFF[b], SOF + Z_OFF[b] + Z_LEN[b])
                    mm = product(o_ps[:, P * b:SEQ], b_hi[:, vs], b_lo[:, vs], b_hi[:, ps], b_lo[:, ps],
                                 b == 0, b == QB - 1)
                mm.then_inc(o_done, 1)

            def v_rows(i):
                pe.wait_ge(taken, 3 + i * S1_PER)
                if not (isinstance(i, int) and i == 0):
                    pe.wait_ge(y_done, 2 * i)
                for b in range(QB):
                    mm = pe.transpose(o_ps[:, P * b:P * (b + 1)], ev[:, 2, P * b:P * (b + 1)], ident[:, :])
                mm.then_inc(vt_done, 1)

            def group(g):
                n = N_GRP + g
                take(n)
                if g == 0:
                    pe.wait_ge(glo_done, 1)
                pe.wait_ge(mlo_done, g + 1)
                wg = slice(GOF + g * P, GOF + (g + 1) * P)
                hi, lo = mean_part(0, g), mean_part(1, g)
                for h in range(2):
                    c = slice(h * HALF, (h + 1) * HALF)
                    mm = product(result(n)[:, h, :], b_hi[:, wg], b_lo[:, wg], hi[:, c], lo[:, c], True, True)
                mm.then_inc(full, 1)

            def pool_part(m):
                t, n = T_MIX + m // 2, N_POOL[m]
                weights(t)
                take(n)
                dense(result(n), t % W_RING, [(PAIRS + k, m % 2 * 4 + k) for k in range(4)], A,
                      (lambda k: (taken, N_GRP + 1 + k - PAIRS)) if m == 0 else None).then_inc(full, 1)

            def pair(i):
                first = isinstance(i, int) and i == 0
                if first:
                    dense(result(0), 0, ALL, A, lambda k: (xlo_done, k + 1),
                          lambda k: (half_lo_done, 1) if k < KT // 2 else (wlo_done, 1)).then_inc(full, 1)
                else:
                    tile(0, i)
                tile(1, i)
                if first:
                    pe.wait_ge(const_made, N_CONST)
                    pe.wait_ge(sq_added, KT)
                    stats(None).then_inc(stat0, 1)
                else:
                    sums(1, i - 1)
                tile(2, i)
                if first:
                    pe.wait_ge(var_done, 1)
                    tile(3, i)
                    pe.wait_ge(taken, 4)
                else:
                    outputs(1, i - 1)
                scores(0, i)
                if not first:
                    tile(3, i)
                v_rows(i)
                tile(4, i)
                tile(5, i)
                sums(0, i)
                tile(6, i)
                outputs(0, i)
                scores(1, i)
                tile(7, i)

            pair(0)
            with pe.Fori(1, PAIRS - 1) as i:
                pair(i)
            pair(PAIRS - 1)
            for g in range(GROUPS):
                group(g)
            pool_part(0)
            pool_part(1)
            sums(1, PAIRS - 1)
            pool_part(2)
            pool_part(3)
            outputs(1, PAIRS - 1)

            pe.wait_ge(past_in, 32)
            for b in range(2):
                for p in range(PAIRS):
                    pe.matmul(zs_ps[:, b * ZS + p * 2 * DEC:b * ZS + (p + 1) * 2 * DEC],
                              ckt[:, p, P * b:P * (b + 1)], qbd[:, p, :],
                              start=(b == 0 and p == 0), stop=False, skip_group_check=True)
            for p in range(PAIRS):
                mm = pe.matmul(zs2_ps[:, p * 2 * DEC:(p + 1) * 2 * DEC], kst[:, p, :], qbd[:, p, :],
                               start=(p == 0), stop=False, skip_group_check=True)
            mm.then_inc(z_done, 1)
            take(N_VS)
            for p in range(PAIRS):
                mm = pe.transpose(psum[0:DEC, 2 * result_slot(N_VS), P * p:P * (p + 1)], vst[:, p, :], ident[:, :])
            mm.then_inc(full, 1)

            pool_part(4)
            pool_part(5)
            pe.wait_ge(spm_done, HEADS * QB + 1)
            tri, one = negtri[:, :].bitcast(F32), negone[:, :].bitcast(F32)
            for b in range(2):
                z = zs_ps[:, b * ZS:(b + 1) * ZS]
                pe.matmul(z, tri, work[:, b * ZS:(b + 1) * ZS], start=False, stop=False, skip_group_check=True)
                if b == 0:
                    pe.matmul(z, one, work[:, ZS:2 * ZS], start=False, stop=False, skip_group_check=True)
                pe.matmul(z, one[0:DEC, :], work_s2, start=False, stop=True, skip_group_check=True)
            pe.matmul(zs2_ps, tri[0:DEC, 0:DEC], work_s2, start=False, stop=True,
                      skip_group_check=True).then_inc(c_done, 1)
            pool_part(6)
            pe.wait_ge(pm_done, HEADS * QB + 1)
            pe.wait_ge(taken, N_VS + 1)
            for p in range(PAIRS):
                o = os_ps[:, p * 2 * DEC:(p + 1) * 2 * DEC]
                q = slice(p * 2 * DEC, (p + 1) * 2 * DEC)
                for b in range(2):
                    pe.matmul(o, cvn[:, b, P * p:P * (p + 1)], work[:, b * ZS:(b + 1) * ZS][:, q],
                              start=(b == 0), stop=False, skip_group_check=True)
                mm = pe.matmul(o, vsn[:, P * p:P * (p + 1)], work_s2[:, q], start=False, stop=True,
                               skip_group_check=True)
            mm.then_inc(o_done, 1)
            pool_part(7)
            for m in range(KT):
                t, n = T_MIX + KT // 2 + m // 2, N_ATT + m
                weights(t)
                take(n)
                if m == 0:
                    pe.wait_ge(yblo_done, 2)
                dense(result(n), t % W_RING, [(k, m % 2 * 4 + k) for k in range(4)], A).then_inc(full, 1)
            for m in range(KT):
                t, n = T_OUT + m, N_OUT + m
                weights(t)
                take(n)
                dense(result(n), t % W_RING, ALL, B,
                      (lambda k: (blo_done, k + 1)) if m == 0 else None).then_inc(full, 1)

            def mlp(c, j):
                t, n, up = T_MLP + j, mlp_result(j), j % MLP_PER < KT
                weights(t, c, MLP_PER)
                if isinstance(c, int) and c == 0:
                    take(n)
                else:
                    pe.wait_ge(taken, n - (2 if j == 3 else 3) + c * MLP_PER)
                ready = None
                if isinstance(c, int) and c == 0 and j == 0:
                    ready = lambda k: (xlo_done, KT + k + 1)
                if j == KT:
                    ready = lambda k: (hlo_done, c * KT + (k + 1))
                dense(result(n), t % W_RING, ALL, A if up else B, ready).then_inc(full, 1)

            mlp(0, 0)
            take(N_STAT1)
            pe.wait_ge(sq_added, 2 * KT)
            stats(N_STAT1).then_inc(full, 1)
            with pe.Fori(0, CHUNKS - 1) as c:
                for j in range(1, MLP_PER + 1):
                    mlp(c, j)
            for j in range(1, MLP_PER):
                mlp(CHUNKS - 1, j)
            for m in range(KT):
                t, n = T_PLE + m, gate_result(m)
                weights(t)
                take(n)
                dense(result(n), t % W_RING, ALL, A,
                      (lambda k: (xlo_done, 2 * KT + k + 1)) if m == 0 else None).then_inc(full, 1)
                if m == 0:
                    take(N_STAT2)
                    pe.wait_ge(sq_added, 3 * KT)
                    stats(N_STAT2).then_inc(full, 1)
                    pe.wait_ge(ptlo_done, 2)
                n = N_PLE + 2 * m + 1
                take(n)
                for k in range(PLE // P):
                    wsl = slice(wp_of + k * D_MODEL + m * P, wp_of + k * D_MODEL + (m + 1) * P)
                    for h in range(2):
                        c = slice(pr_of + k * TOK + h * HALF, pr_of + k * TOK + (h + 1) * HALF)
                        mm = product(result(n)[:, h, :], b_hi[:, wsl], b_lo[:, wsl], b_hi[:, c], b_lo[:, c],
                                     k == 0, k == 1)
                mm.then_inc(full, 1)
            take(N_STAT3)
            pe.wait_ge(sq_added, 4 * KT)
            stats(N_STAT3).then_inc(full, 1)

        @block.vector
        def _(dve):
            own = [0]

            def link(ins):
                own[0] += 1
                ins.then_inc(dve_own, 1)
                dve.wait_ge(dve_own, own[0])

            def split(t, i=0, per=0):
                s = t % W_RING
                dve.wait_ge(whi_done, t + 1 + i * per)
                dve.tensor_tensor(w_lo[:, s, :, :].rearrange("p k c -> p (k c)"), raw[:, t % RAW_RING, :],
                                  w_hi[:, s, :, :].rearrange("p k c -> p (k c)"), ALU.subtract).then_inc(wlo_done, 1)

            def input_lo(k, g, n0):
                dve.wait_ge(xhi_done, n0 + k + 1)
                dve.scalar_tensor_tensor(out=cols(a_lo, k), in0=xt[:, k, :], scalar=g[:, k:k + 1],
                                         in1=cols(a_hi, k), op0=ALU.mult, op1=ALU.subtract).then_inc(xlo_done, 1)

            def add_square(k, n0):
                dve.wait_ge(sq_done, n0 - POOL_SQUARES + k + 1)
                e = ev[:, 1 + k % 2, 0:TOK]
                if k == 0:
                    dve.tensor_copy(acc, e).then_inc(sq_added, 1)
                else:
                    dve.wait_ge(sq_added, n0 + k)
                    dve.tensor_tensor(acc, acc, e, ALU.add).then_inc(sq_added, 1)

            def embeddings_lo():
                dve.wait_ge(pt_done, 2)
                dve.tensor_tensor(b_lo[:, pr_of:pr_of + 2 * TOK].rearrange("p (k t) -> p k t", k=2), p_raw,
                                  b_hi[:, pr_of:pr_of + 2 * TOK].rearrange("p (k t) -> p k t", k=2),
                                  ALU.subtract).then_inc(ptlo_done, 1)
                dve.tensor_tensor(b_lo[:, wp_of:wp_of + 4 * SEQ].rearrange("p (k t) -> p k t", k=4), wp_raw,
                                  b_hi[:, wp_of:wp_of + 4 * SEQ].rearrange("p (k t) -> p k t", k=4),
                                  ALU.subtract).then_inc(ptlo_done, 1)

            def inverse_rms(sums, nth, signal):
                dve.tensor_scalar(halves(var), sums, -1.0 / D_MODEL, EPS, ALU.mult, ALU.add).then_inc(signal, 1)
                dve.wait_ge(root_done, nth)
                r, t = ev[:, 1, 0:TOK], ev[:, 2, 0:TOK]
                link(dve.scalar_tensor_tensor(out=t, in0=r, scalar=-0.5, in1=r, op0=ALU.mult, op1=ALU.mult))
                link(dve.tensor_tensor(t, t, var, ALU.mult))
                link(dve.scalar_tensor_tensor(out=rn[:, :], in0=t, scalar=1.5, in1=r, op0=ALU.add, op1=ALU.mult))

            def normed(n, out, i=0, per=0, banks=None):
                dve.wait_ge(full, n + 1 + i * per)
                return dve.tensor_tensor(halves(out), result(n) if banks is None else banks, halves(rn[:, :]), ALU.mult)

            def half(n, hi_done, done):
                part = slice(n * D_MODEL // 2, (n + 1) * D_MODEL // 2)
                dve.wait_ge(hi_done, 1)
                dve.tensor_tensor(w_lo[:, 0, :, :].rearrange("p k c -> p (k c)")[:, part], raw[:, 0, part],
                                  w_hi[:, 0, :, :].rearrange("p k c -> p (k c)")[:, part],
                                  ALU.subtract).then_inc(done, 1)

            half(0, half_hi_done, half_lo_done)
            dve.wait_ge(vec_in, 16)
            for k in range(KT):
                input_lo(k, g_mix, 0)
                if k == 1:
                    half(1, whi_done, wlo_done)
                if k == 4:
                    split(1)
            for k in range(POOL_SQUARES, KT):
                add_square(k, 0)
                if k == POOL_SQUARES + 1:
                    split(2)
            dve.wait_ge(ghi_done, 1)
            dve.tensor_tensor(b_lo[:, GOF:GOF + GROUPS * P], ev[:, 0, 0:GROUPS * P],
                              b_hi[:, GOF:GOF + GROUPS * P], ALU.subtract).then_inc(glo_done, 1)
            split(3)
            dve.wait_ge(stat0, 1)
            inverse_rms(psum[:, 6:8, 0:HALF], 1, var_done)

            def stick(hh, i):
                g = 2 * i + hh
                dve.wait_ge(ln_done, g + 1)
                dve.scalar_tensor_tensor(out=work[:, :], in0=z_ps, scalar=0.0, in1=work[:, :],
                                         op0=ALU.max, op1=ALU.add).then_inc(sp_done, 1)

            def stick_lo(hh, i):
                dve.wait_ge(shi_done, 2 * i + hh + 1)
                dve.tensor_tensor(b_lo[:, SOF:SOF + Z_COLS], work[:, :], b_hi[:, SOF:SOF + Z_COLS],
                                  ALU.subtract).then_inc(slo_done, 1)

            def prob_lo(hh, i):
                dve.wait_ge(phi_done, 2 * i + hh + 1)
                dve.tensor_tensor(b_lo[:, SOF:SOF + Z_COLS], work[:, :], b_hi[:, SOF:SOF + Z_COLS],
                                  ALU.subtract).then_inc(plo_done, 1)

            def head_out(hh, i):
                r = slice(DH * hh, DH * hh + DH)
                dve.wait_ge(o_done, 2 * i + hh + 1)
                dve.tensor_copy(ysb[r, i, 0:SEQ], o_ps[r, :]).then_inc(y_done, 1)

            def gate(jj, i):
                j = 4 + jj
                dve.wait_ge(full, j + 1 + i * S1_PER)
                dve.tensor_tensor(halves(gates[:, 4 * i + jj, :]), pair_result(j, i), halves(rn[:, :]), ALU.mult)\
                   .then_inc(taken, 1)

            def mean_lo(g):
                dve.wait_ge(mhi_done, g + 1)
                hi, lo = mean_part(0, g), mean_part(1, g)
                dve.tensor_tensor(lo[:, 0:SEQ], upad[:, g, U_PROMPT:U_STATE], hi[:, 0:SEQ], ALU.subtract)
                dve.tensor_tensor(lo[:, SEQ:TOK], upad[:, g, U_SAMPLE:PADW], hi[:, SEQ:TOK], ALU.subtract)\
                   .then_inc(mlo_done, 1)

            def group_lo(g):
                dve.wait_ge(ghi_done, g + 2)
                dve.scalar_tensor_tensor(out=halves(cols(a_lo, PAIRS + g)), in0=result(N_GRP + g),
                                         scalar=pscale[:, g:g + 1], in1=halves(cols(a_hi, PAIRS + g)),
                                         op0=ALU.mult, op1=ALU.subtract).then_inc(taken, 1)

            def pair(i):
                first = isinstance(i, int) and i == 0
                last = isinstance(i, int) and i == PAIRS - 1
                q, k, v = (ev[:, n, 0:TOK] for n in range(3))
                if not first:
                    split(AHEAD + 0, i, S1_PER)
                dve.wait_ge(full, 1 + i * S1_PER)
                dve.scalar_tensor_tensor(out=halves(q), in0=pair_result(0, i), scalar=DH ** -0.5, in1=halves(rn[:, :]),
                                         op0=ALU.mult, op1=ALU.mult).then_inc(taken, 1)
                dve.wait_ge(taken, 1 + i * S1_PER)
                for h in range(2):
                    r = slice(DH * h, DH * (h + 1))
                    dve.tensor_copy(qbd[r, i, DEC * h:DEC * (h + 1)], q[r, SEQ:TOK])
                dve.wait_ge(qkhi_done, 2 * i + 1)
                dve.tensor_tensor(b_lo[:, QOF:QOF + TOK], q, b_hi[:, QOF:QOF + TOK], ALU.subtract)\
                   .then_inc(qklo_done, 1)
                split(AHEAD + 1, i, S1_PER)
                if not first:
                    dve.wait_ge(kv_out[0], 16 * i)
                normed(1, k, i, S1_PER, pair_result(1, i)).then_inc(taken, 1)
                dve.wait_ge(taken, 2 + i * S1_PER)
                dve.tensor_copy(kst[:, i, :], k[:, SEQ:TOK])
                dve.wait_ge(qkhi_done, 2 * i + 2)
                dve.tensor_tensor(b_lo[:, KOF:KOF + TOK], k, b_hi[:, KOF:KOF + TOK], ALU.subtract)\
                   .then_inc(qklo_done, 1)
                split(AHEAD + 2, i, S1_PER)
                if not first:
                    prob_lo(1, i - 1)
                if not first:
                    dve.wait_ge(kv_out[1], 16 * i)
                normed(2, v, i, S1_PER, pair_result(2, i)).then_inc(taken, 1)
                dve.wait_ge(taken, 3 + i * S1_PER)
                dve.tensor_copy(vst[:, i, :], v[:, SEQ:TOK])
                if not first:
                    head_out(1, i - 1)
                    stick(0, i)
                    split(AHEAD + 3, i, S1_PER)
                dve.wait_ge(full, 4 + i * S1_PER)
                u = upad[:, i, :]
                dve.tensor_tensor(u[:, U_PROMPT:U_PROMPT + HALF], pair_result(3, i)[:, 0, :], rn[:, 0:HALF], ALU.mult)
                dve.tensor_tensor(u[:, U_PROMPT + HALF:U_STATE], pair_result(3, i)[:, 1, 0:SEQ - HALF],
                                  rn[:, HALF:SEQ], ALU.mult)
                dve.tensor_tensor(u[:, U_SAMPLE:PADW], pair_result(3, i)[:, 1, SEQ - HALF:HALF],
                                  rn[:, SEQ:TOK], ALU.mult).then_inc(taken, 1)
                if first:
                    stick(0, i)
                    split(AHEAD + 3)
                stick_lo(0, i)
                dve.wait_ge(vhi_done, i + 1)
                dve.tensor_tensor(b_lo[:, VOF:VOF + SEQ], o_ps, b_hi[:, VOF:VOF + SEQ], ALU.subtract)\
                   .then_inc(vlo_done, 1)
                split(AHEAD + 4, i, S1_PER)
                gate(0, i)
                split(AHEAD + 5, i, S1_PER)
                if last:
                    dve.wait_ge(mean_done, GROUPS)
                gate(1, i)
                split(AHEAD + 6, i, S1_PER)
                if last:
                    mean_lo(0)
                prob_lo(0, i)
                gate(2, i)
                head_out(0, i)
                split(AHEAD + 7, i, S1_PER)
                stick(1, i)
                if last:
                    mean_lo(1)
                stick_lo(1, i)
                gate(3, i)
                if last:
                    mean_lo(2)
                    mean_lo(3)
                    for s in kv_out:
                        dve.wait_ge(s, 16 * PAIRS)

            pair(0)
            with dve.Fori(1, PAIRS - 1) as i:
                pair(i)
            pair(PAIRS - 1)

            ah = a_hi[:, 0:PAIRS * TOK].rearrange("p (k t) -> p k t", k=PAIRS)
            al = a_lo[:, 0:PAIRS * TOK].rearrange("p (k t) -> p k t", k=PAIRS)

            def heads_lo(nth, c):
                dve.wait_ge(ybhi_done, nth)
                dve.tensor_tensor(al[:, :, c], ysb[:, :, c], ah[:, :, c], ALU.subtract).then_inc(yblo_done, 1)

            def gated(n, g, nth):
                dve.wait_ge(sig_done, nth)
                dve.wait_ge(full, n + 1)
                dve.tensor_tensor(halves(gates[:, g, :]), result(n), halves(gates[:, g, :]), ALU.mult)\
                   .then_inc(taken, 1)

            for g in range(GROUPS):
                group_lo(g)
            split(T_MIX + AHEAD)
            gated(N_POOL[0], 0, 1)
            gated(N_POOL[1], 1, 2)
            split(T_MIX + 1 + AHEAD)
            prob_lo(1, PAIRS - 1)
            gated(N_POOL[2], 2, 3)
            gated(N_POOL[3], 3, 4)
            split(T_MIX + 2 + AHEAD)
            head_out(1, PAIRS - 1)
            heads_lo(1, slice(0, SEQ))
            dve.wait_ge(full, N_VS + 1)
            dve.tensor_copy(vsn, psum[0:DEC, 2 * result_slot(N_VS), :]).then_inc(taken, 1)
            dve.wait_ge(ln_done, HEADS + 1)
            dve.scalar_tensor_tensor(out=work_s, in0=zs_ps, scalar=0.0, in1=work_s, op0=ALU.max, op1=ALU.add)
            dve.scalar_tensor_tensor(out=work_s2, in0=zs2_ps, scalar=0.0, in1=work_s2,
                                     op0=ALU.max, op1=ALU.add).then_inc(sp_done, 1)
            gated(N_POOL[4], 4, 5)
            gated(N_POOL[5], 5, 6)
            split(T_MIX + 3 + AHEAD)
            dve.wait_ge(o_done, HEADS + 1)
            for h in range(2):
                r = slice(DH * h, DH * (h + 1))
                o = os_ps.rearrange("p (k q) -> p k q", k=PAIRS)
                dve.tensor_copy(ysb[r, :, SEQ:TOK], o[r, :, DEC * h:DEC * (h + 1)]).then_inc(y_done, 1)
            heads_lo(2, slice(SEQ, TOK))
            gated(N_POOL[6], 6, 7)
            gated(N_POOL[7], 7, 8)
            for m in range(KT):
                if m % 2 == 0:
                    split(T_MIX + KT // 2 + m // 2 + AHEAD)
                gated(N_ATT + m, KT + m, KT + m + 1)
                dve.wait_ge(taken, N_ATT + m + 1)
                dve.tensor_tensor(gates[:, m, :], gates[:, m, :], gates[:, KT + m, :], ALU.add)\
                   .then_inc(mix_done, 1)
                dve.wait_ge(bhi_done, m + 1)
                dve.tensor_tensor(cols(b_lo, m), gates[:, m, :], cols(b_hi, m), ALU.subtract)\
                   .then_inc(blo_done, 1)

            def add_residual(n, m, i=0, per=0):
                dve.wait_ge(full, n + 1 + i * per)
                dve.tensor_tensor(halves(xt[:, m, :]), result(n), halves(xt[:, m, :]), ALU.add).then_inc(taken, 1)

            for m in range(KT):
                split(T_OUT + m + AHEAD)
                add_residual(N_OUT + m, m)
                input_lo(m, g_mlp, KT)
                add_square(m, KT)

            def mlp(c, j, last=False):
                split(T_MLP + j + AHEAD, c, MLP_PER)
                n = mlp_result(j)
                if isinstance(c, int) and c == 0 and j == 0:
                    dve.wait_ge(full, N_STAT1 + 1)
                    inverse_rms(result(N_STAT1), 2, taken)
                if j % MLP_PER < KT:
                    k = j % MLP_PER
                    h, nth = work[:, (k % 2) * TOK:(k % 2 + 1) * TOK], j // MLP_PER * KT + k
                    if k >= 2:
                        dve.wait_ge(hlo_done, c * KT + (nth - 1))
                    normed(n, h, c, MLP_PER).then_inc(taken, 1)
                    dve.wait_ge(taken, taken_by(n) + c * MLP_PER)
                    dve.scalar_tensor_tensor(out=h, in0=h, scalar=0.0, in1=h, op0=ALU.max, op1=ALU.mult)\
                       .then_inc(h_done, 1)
                    dve.wait_ge(hhi_done, c * KT + (nth + 1))
                    dve.tensor_tensor(cols(b_lo, k), h, cols(b_hi, k), ALU.subtract).then_inc(hlo_done, 1)
                else:
                    m = j - KT
                    add_residual(n, m, c, MLP_PER)
                    if last:
                        input_lo(m, g_ple, 2 * KT)
                        add_square(m, 2 * KT)

            mlp(0, 0)
            with dve.Fori(0, CHUNKS - 1) as c:
                for j in range(1, MLP_PER + 1):
                    mlp(c, j)
            for j in range(1, MLP_PER):
                mlp(CHUNKS - 1, j, last=True)
            embeddings_lo()
            dve.wait_ge(full, N_STAT2 + 1)
            inverse_rms(result(N_STAT2), 3, taken)
            for m in range(KT):
                n, s = gate_result(m), gates[:, KT + m, :]
                if T_PLE + m + AHEAD < N_TILES:
                    split(T_PLE + m + AHEAD)
                normed(n, s).then_inc(taken, 1)
                n = N_PLE + 2 * m + 1
                dve.wait_ge(psig_done, m + 1)
                dve.wait_ge(full, n + 1)
                dve.tensor_tensor(halves(s), result(n), halves(s), ALU.mult).then_inc(taken, 1)
                dve.wait_ge(taken, n + 1)
                dve.tensor_tensor(xt[:, m, :], xt[:, m, :], s, ALU.add).then_inc(res_done, 1)
                add_square(m, 3 * KT)
            dve.wait_ge(full, N_STAT3 + 1)
            inverse_rms(result(N_STAT3), 4, taken)
            for m in range(KT):
                dve.scalar_tensor_tensor(out=xt[:, m, :], in0=xt[:, m, :], scalar=g_fin[:, m:m + 1],
                                         in1=rn[:, :], op0=ALU.mult, op1=ALU.mult).then_inc(fin_done, 1)


_SHAPES = [("y_t", (KT, P, TOK)), ("k_t", (PAIRS, P, TOK)), ("v_t", (PAIRS, P, TOK)),
           ("pool_t", (2, P, GROUPS, STATE))]


def kernel(x_prompt, x_sample, cache_k, cache_v, state_pool, p_prompt, p_sample,
           g_mix, w_in, b_gate, w_pool_grp, pool_scale, w_pool_up, w_sb_up, w_out,
           g_mlp, w_up, w_down, g_ple, w_ple_gate, w_ple_proj, g_final):
    import concourse.bacc as bacc
    from concourse.bass_utils import run_bass_kernel_spmd

    def rows(a):
        return np.ascontiguousarray(a)

    def column_tiles(w, starts):
        return [w[:, c:c + P].reshape(KT, P, P).transpose(1, 0, 2).reshape(P, KT * P) for c in starts]

    def features_first(prompt, sample):
        return np.concatenate([prompt, sample], axis=0).T

    def per_partition(v):
        return v.reshape(-1, P).T

    (x_prompt, x_sample, cache_k, cache_v, state_pool, p_prompt, p_sample, g_mix, w_in, b_gate, w_pool_grp,
     pool_scale, w_pool_up, w_sb_up, w_out, g_mlp, w_up, w_down, g_ple, w_ple_gate, w_ple_proj, g_final) = (
        np.asarray(a) for a in (x_prompt, x_sample, cache_k, cache_v, state_pool, p_prompt, p_sample, g_mix,
                                w_in, b_gate, w_pool_grp, pool_scale, w_pool_up, w_sb_up, w_out, g_mlp, w_up,
                                w_down, g_ple, w_ple_gate, w_ple_proj, g_final))
    W = HEADS * DH
    tiles = []
    for p in range(PAIRS):
        starts = [W + P * p, 2 * W + P * p, 3 * W + P * p, P * p] + [4 * W + P * (4 * p + j) for j in range(4)]
        tiles += column_tiles(w_in[0], starts)
    every = [P * m for m in range(KT)]
    for w in (w_pool_up[0], w_sb_up[0]):
        tiles += [w[:, c:c + 2 * P].reshape(4, P, 2, P).transpose(1, 2, 0, 3).reshape(P, KT * P)
                  for c in every[::2]]
    tiles += column_tiles(w_out[0], every)
    for c in range(CHUNKS):
        tiles += column_tiles(w_up[0], [D_MODEL * c + a for a in every])
        tiles += column_tiles(w_down[0, D_MODEL * c:D_MODEL * (c + 1)], every)
    tiles += column_tiles(w_ple_gate[0], every)
    arrays = {
        "w_tiles": np.stack(tiles),
        "x_t": rows(features_first(x_prompt[0], x_sample[0]).reshape(KT, P, TOK)),
        "p_t": rows(features_first(p_prompt[0, 0], p_sample[0, 0]).reshape(PLE // P, P, TOK).transpose(1, 0, 2)),
        "ck_t": rows(cache_k[0, 0].reshape(PAST, PAIRS, P).transpose(2, 1, 0)),
        "cv": rows(cache_v[0, 0].reshape(PAST // P, P, W).transpose(1, 0, 2)),
        "state_t": rows(state_pool[0, 0].reshape(STATE, GROUPS, P).transpose(2, 1, 0)),
        "w_grp": rows(w_pool_grp[0].transpose(1, 0, 2).reshape(P, GROUPS * P)),
        "w_ple": rows(w_ple_proj[0].reshape(PLE // P, P, 2, SEQ).transpose(1, 0, 2, 3).reshape(P, 4, SEQ)),
        "vecs": rows(np.concatenate([per_partition(a) for a in (g_mix[0], g_mlp[0], g_ple[0], g_final,
                                                                 b_gate[0], pool_scale[0])], axis=1)),
    }
    nc = bacc.Bacc("TRN2", target_bir_lowering=False, num_devices=1)
    ins = [nc.dram_tensor(n, a.shape, F32, kind="ExternalInput").ap() for n, a in arrays.items()]
    outs = [nc.dram_tensor(n, s, F32, kind="ExternalOutput").ap() for n, s in _SHAPES]
    hybrid_step_kernel(nc, *ins, *outs)
    r = run_bass_kernel_spmd(nc, [arrays], core_ids=[0]).results[0]
    y, k, v, pool = (r[n] for n, _ in _SHAPES)
    y = y.reshape(D_MODEL, TOK).T
    k, v = (a.reshape(W, TOK).T.reshape(TOK, HEADS, DH) for a in (k, v))
    pool = pool.transpose(0, 3, 2, 1).reshape(2, STATE, GROUPS * P)
    return (rows(y[None, :SEQ]), rows(y[None, SEQ:]), rows(k[None, None, :SEQ]), rows(v[None, None, :SEQ]),
            rows(pool[0][None, None]), rows(k[None, None, SEQ:]), rows(v[None, None, SEQ:]),
            rows(pool[1][None, None]))
```
